# Optimizing a Trainium2 kernel written in Bass

```python
import math
import jax
import jax.numpy as jnp
from jax import lax
import numpy as np
import jax, jax.numpy as jnp

D_MODEL = 1024
BATCH = 1
SEQ = 256
DEPTH = 4

N_MIXERS = 3
N_GDN = (DEPTH + 2) // 3
N_SB = (DEPTH + 1) // 3
N_DSA = DEPTH // 3

D_FF = 2816
NORM_EPS = 1e-6
ROPE_THETA = 500000.0
Q_BLOCK = 128

GDN_HEADS = 8
GDN_HEAD_DIM = 128
GDN_DIM = GDN_HEADS * GDN_HEAD_DIM
GDN_CONV = 4
GDN_CHUNK = 64
GDN_IN = 4 * GDN_DIM + 2 * GDN_HEADS

SB_HEADS = 8
SB_HEAD_DIM = 128
SB_DIM = SB_HEADS * SB_HEAD_DIM

DSA_HEADS = 8
DSA_Q_RANK = 384
DSA_KV_RANK = 256
DSA_ROPE_DIM = 32
DSA_NOPE_DIM = 96
DSA_QK_DIM = DSA_ROPE_DIM + DSA_NOPE_DIM
DSA_V_DIM = 128
DSA_IDX_HEADS = 8
DSA_IDX_DIM = 64
DSA_TOPK_MAX = 256
DSA_IN = DSA_Q_RANK + DSA_KV_RANK + DSA_ROPE_DIM + DSA_IDX_DIM + DSA_IDX_HEADS


def rmsnorm(x, g):
    xf = x.astype(jnp.float32)
    y = xf * lax.rsqrt(jnp.mean(xf * xf, axis=-1, keepdims=True) + NORM_EPS)
    return (y * g.astype(jnp.float32)).astype(x.dtype)

def l2norm(x):
    return x * lax.rsqrt(jnp.sum(x * x, axis=-1, keepdims=True) + NORM_EPS)

def rope(x, pos):
    r = x.shape[-1]
    half = r // 2
    inv_freq = ROPE_THETA ** (-jnp.arange(half, dtype=jnp.float32) * (2.0 / r))
    ang = pos.astype(jnp.float32)[:, None] * inv_freq[None, :]
    shape = (pos.shape[0],) + (1,) * (x.ndim - 3) + (half,)
    cos = jnp.cos(ang).reshape(shape)
    sin = jnp.sin(ang).reshape(shape)
    xf = x.astype(jnp.float32)
    x1, x2 = xf[..., :half], xf[..., half:]
    return jnp.concatenate([x1 * cos - x2 * sin, x2 * cos + x1 * sin], axis=-1).astype(x.dtype)

def partial_rope(x, pos):
    r = x.shape[-1] // 4
    return jnp.concatenate([rope(x[..., :r], pos), x[..., r:]], axis=-1)

def swiglu(h, w_gu, w_down):
    gate, up = jnp.split(h @ w_gu, 2, axis=-1)
    return (jax.nn.silu(gate) * up) @ w_down

def causal_depthwise_conv(x, w):
    kw, ch = w.shape
    return lax.conv_general_dilated(
        x, w[:, None, :].astype(x.dtype), window_strides=(1,), padding=[(kw - 1, 0)],
        dimension_numbers=('NWC', 'WIO', 'NWC'), feature_group_count=ch)

def to_blocks(t, block):
    b, s = t.shape[:2]
    return jnp.swapaxes(t.reshape((b, s // block, block) + t.shape[2:]), 0, 1)

def from_blocks(t):
    nb, b, blk = t.shape[:3]
    return jnp.swapaxes(t, 0, 1).reshape((b, nb * blk) + t.shape[3:])

def chunk_gated_delta_rule(q, k, v, g, beta):
    bsz, seq, nh, dk = q.shape
    dv = v.shape[-1]
    c = GDN_CHUNK
    n = seq // c

    def chunks(t):
        return jnp.moveaxis(t.reshape((bsz, n, c, nh) + t.shape[3:]), 3, 1)

    q, k, v, g, beta = chunks(q), chunks(k), chunks(v), chunks(g), chunks(beta)
    g_cum = jnp.cumsum(g, axis=-1)
    incl = jnp.tril(jnp.ones((c, c), dtype=bool))
    strict = jnp.tril(jnp.ones((c, c), dtype=bool), -1)
    seg = g_cum[..., :, None] - g_cum[..., None, :]
    decay = jnp.where(incl, jnp.exp(jnp.where(incl, seg, 0.0)), 0.0)
    kk = jnp.einsum('bhnid,bhnjd->bhnij', k, k)
    lower = jnp.where(strict, beta[..., :, None] * kk * decay, 0.0)
    eye = jnp.eye(c, dtype=jnp.float32)
    rhs = jnp.concatenate([v * beta[..., None], k * (beta * jnp.exp(g_cum))[..., None]], axis=-1)
    sol = lax.linalg.triangular_solve(lower + eye, rhs, left_side=True, lower=True, unit_diagonal=True)
    u_in, w = sol[..., :dv], sol[..., dv:]
    qk = jnp.einsum('bhnid,bhnjd->bhnij', q, k) * decay
    q_dec = q * jnp.exp(g_cum)[..., None]
    k_dec = k * jnp.exp(g_cum[..., -1:] - g_cum)[..., None]
    g_tot = jnp.exp(g_cum[..., -1])
    xs = tuple(jnp.moveaxis(t, 2, 0) for t in (u_in, w, qk, q_dec, k_dec, g_tot))

    def step(state, inp):
        u_c, w_c, qk_c, qd_c, kd_c, gt_c = inp
        u = u_c - jnp.einsum('bhck,bhkv->bhcv', w_c, state)
        o = jnp.einsum('bhck,bhkv->bhcv', qd_c, state) + jnp.einsum('bhcj,bhjv->bhcv', qk_c, u)
        state = state * gt_c[..., None, None] + jnp.einsum('bhck,bhcv->bhkv', kd_c, u)
        return state, o

    state0 = jnp.zeros((bsz, nh, dk, dv), jnp.float32)
    _, o = lax.scan(step, state0, xs)
    return jnp.transpose(o, (1, 0, 3, 2, 4)).reshape(bsz, seq, nh, dv)

def gated_deltanet(h, w_in, conv_w, a_log, dt_bias, norm_g, w_out):
    bsz, seq, _ = h.shape
    proj = h @ w_in
    qkv = jax.nn.silu(causal_depthwise_conv(proj[..., :3 * GDN_DIM], conv_w))
    z = proj[..., 3 * GDN_DIM:4 * GDN_DIM]
    b_logit = proj[..., 4 * GDN_DIM:4 * GDN_DIM + GDN_HEADS].astype(jnp.float32)
    a = proj[..., 4 * GDN_DIM + GDN_HEADS:].astype(jnp.float32)

    def heads(t):
        return t.reshape(bsz, seq, GDN_HEADS, GDN_HEAD_DIM).astype(jnp.float32)

    q, k, v = (heads(t) for t in jnp.split(qkv, 3, axis=-1))
    q = l2norm(q) * GDN_HEAD_DIM ** -0.5
    k = l2norm(k)
    beta = jax.nn.sigmoid(b_logit)
    g = -jnp.exp(a_log.astype(jnp.float32)) * jax.nn.softplus(a + dt_bias.astype(jnp.float32))
    o = chunk_gated_delta_rule(q, k, v, g, beta)
    o = rmsnorm(o, norm_g) * jax.nn.silu(heads(z))
    return o.reshape(bsz, seq, GDN_DIM).astype(h.dtype) @ w_out

def stick_breaking_attention(h, w_in, w_out):
    bsz, seq, _ = h.shape
    q, k, v = (t.reshape(bsz, seq, SB_HEADS, SB_HEAD_DIM).astype(jnp.float32)
               for t in jnp.split(h @ w_in, 3, axis=-1))
    scale = SB_HEAD_DIM ** -0.5
    key_pos = jnp.arange(seq)

    def block(args):
        q_blk, t0 = args
        z = jnp.einsum('bqhd,bkhd->bhqk', q_blk, k) * scale
        q_pos = t0 + jnp.arange(Q_BLOCK)
        earlier = key_pos[None, :] < q_pos[:, None]
        log_beta = jax.nn.log_sigmoid(z)
        log_fail = jnp.where(earlier, log_beta - z, 0.0)
        log_a = log_beta + lax.cumsum(log_fail, axis=3, reverse=True) - log_fail
        att = jnp.where(earlier, jnp.exp(log_a), 0.0)
        return jnp.einsum('bhqk,bkhd->bqhd', att, v)

    starts = jnp.arange(seq // Q_BLOCK, dtype=jnp.int32) * Q_BLOCK
    o = from_blocks(lax.map(block, (to_blocks(q, Q_BLOCK), starts)))
    return o.reshape(bsz, seq, SB_DIM).astype(h.dtype) @ w_out

def dsa_sparse_attention(h, w_in, cq_g, ckv_g, kidx_g, w_uq, w_qidx, w_uk, w_uv, w_out):
    bsz, seq, _ = h.shape
    topk = min(DSA_TOPK_MAX, seq // 4)
    pos = jnp.arange(seq)
    proj = h @ w_in
    o1 = DSA_Q_RANK
    o2 = o1 + DSA_KV_RANK
    o3 = o2 + DSA_ROPE_DIM
    o4 = o3 + DSA_IDX_DIM
    c_q = rmsnorm(proj[..., :o1], cq_g)
    c_kv = rmsnorm(proj[..., o1:o2], ckv_g)
    k_rope = rope(proj[..., o2:o3], pos)
    k_idx = partial_rope(rmsnorm(proj[..., o3:o4], kidx_g), pos).astype(jnp.float32)
    w_idx = proj[..., o4:].astype(jnp.float32) * (DSA_IDX_HEADS ** -0.5 * DSA_IDX_DIM ** -0.5)
    q = (c_q @ w_uq).reshape(bsz, seq, DSA_HEADS, DSA_QK_DIM)
    q_rope = rope(q[..., :DSA_ROPE_DIM], pos)
    q_nope = q[..., DSA_ROPE_DIM:]
    q_idx = partial_rope((c_q @ w_qidx).reshape(bsz, seq, DSA_IDX_HEADS, DSA_IDX_DIM), pos)
    q_abs = jnp.einsum('bshn,chn->bshc', q_nope, w_uk.reshape(DSA_KV_RANK, DSA_HEADS, DSA_NOPE_DIM))
    q_lat = jnp.concatenate([q_abs, q_rope], axis=-1).astype(jnp.float32)
    k_lat = jnp.concatenate([c_kv, k_rope], axis=-1).astype(jnp.float32)
    scale = DSA_QK_DIM ** -0.5
    batch_ix = jnp.arange(bsz)[:, None, None]

    def block(args):
        qi, wi, ql, t0 = args
        q_pos = t0 + jnp.arange(Q_BLOCK)
        logits = jnp.einsum('bqhd,bkd->bqhk', qi, k_idx)
        score = jnp.einsum('bqh,bqhk->bqk', wi, jax.nn.relu(logits))
        score = jnp.where(pos[None, None, :] <= q_pos[None, :, None], score, -jnp.inf)
        _, idx = lax.top_k(score, topk)
        sel = k_lat[batch_ix, idx]
        att = jnp.einsum('bqhr,bqkr->bqhk', ql, sel) * scale
        att = jnp.where((idx <= q_pos[None, :, None])[:, :, None, :], att, -jnp.inf)
        p = jax.nn.softmax(att, axis=-1)
        return jnp.einsum('bqhk,bqkc->bqhc', p, sel[..., :DSA_KV_RANK])

    starts = jnp.arange(seq // Q_BLOCK, dtype=jnp.int32) * Q_BLOCK
    o_lat = from_blocks(lax.map(block, (to_blocks(q_idx.astype(jnp.float32), Q_BLOCK),
                                        to_blocks(w_idx, Q_BLOCK),
                                        to_blocks(q_lat, Q_BLOCK), starts)))
    o = jnp.einsum('bshc,chv->bshv', o_lat,
                   w_uv.reshape(DSA_KV_RANK, DSA_HEADS, DSA_V_DIM).astype(jnp.float32))
    return o.reshape(bsz, seq, DSA_HEADS * DSA_V_DIM).astype(h.dtype) @ w_out

def first_inputs(seed: int = 0) -> dict:
    key = jax.random.key(seed)
    ks = jax.random.split(key, 26)
    f32 = jnp.float32

    def dense(k, shape):
        return jax.random.normal(k, shape, f32) * shape[-2] ** -0.5

    def gain(k, shape):
        return 1.0 + 0.02 * jax.random.normal(k, shape, f32)

    x = jax.random.normal(ks[0], (BATCH, SEQ, D_MODEL), f32)
    dt = jnp.exp(jax.random.uniform(ks[12], (N_GDN, GDN_HEADS), f32, math.log(1e-3), math.log(1e-1)))
    return {
        'x': x,
        'ffn1_norm': gain(ks[1], (DEPTH, D_MODEL)),
        'ffn1_w_gu': dense(ks[2], (DEPTH, D_MODEL, 2 * D_FF)),
        'ffn1_w_down': dense(ks[3], (DEPTH, D_FF, D_MODEL)),
        'mix_norm': gain(ks[4], (DEPTH, D_MODEL)),
        'ffn2_norm': gain(ks[5], (DEPTH, D_MODEL)),
        'ffn2_w_gu': dense(ks[6], (DEPTH, D_MODEL, 2 * D_FF)),
        'ffn2_w_down': dense(ks[7], (DEPTH, D_FF, D_MODEL)),
        'gdn_w_in': dense(ks[8], (N_GDN, D_MODEL, GDN_IN)),
        'gdn_conv': jax.random.normal(ks[10], (N_GDN, GDN_CONV, 3 * GDN_DIM), f32) * GDN_CONV ** -0.5,
        'gdn_a_log': jnp.log(jax.random.uniform(ks[11], (N_GDN, GDN_HEADS), f32, 1.0, 16.0)),
        'gdn_dt_bias': dt + jnp.log(-jnp.expm1(-dt)),
        'gdn_norm': gain(ks[13], (N_GDN, GDN_HEAD_DIM)),
        'gdn_w_out': dense(ks[9], (N_GDN, GDN_DIM, D_MODEL)),
        'sb_w_in': dense(ks[14], (N_SB, D_MODEL, 3 * SB_DIM)),
        'sb_w_out': dense(ks[15], (N_SB, SB_DIM, D_MODEL)),
        'dsa_w_in': dense(ks[16], (N_DSA, D_MODEL, DSA_IN)),
        'dsa_cq_norm': gain(ks[17], (N_DSA, DSA_Q_RANK)),
        'dsa_ckv_norm': gain(ks[18], (N_DSA, DSA_KV_RANK)),
        'dsa_kidx_norm': gain(ks[19], (N_DSA, DSA_IDX_DIM)),
        'dsa_w_uq': dense(ks[20], (N_DSA, DSA_Q_RANK, DSA_HEADS * DSA_QK_DIM)),
        'dsa_w_qidx': dense(ks[21], (N_DSA, DSA_Q_RANK, DSA_IDX_HEADS * DSA_IDX_DIM)),
        'dsa_w_uk': dense(ks[22], (N_DSA, DSA_KV_RANK, DSA_HEADS * DSA_NOPE_DIM)),
        'dsa_w_uv': dense(ks[23], (N_DSA, DSA_KV_RANK, DSA_HEADS * DSA_V_DIM)),
        'dsa_w_out': dense(ks[24], (N_DSA, DSA_HEADS * DSA_V_DIM, D_MODEL)),
        'final_norm': gain(ks[25], (D_MODEL,)),
    }

def first_block(x, ffn1_norm, ffn1_w_gu, ffn1_w_down, mix_norm, ffn2_norm, ffn2_w_gu, ffn2_w_down,
              gdn_w_in, gdn_conv, gdn_a_log, gdn_dt_bias, gdn_norm, gdn_w_out,
              sb_w_in, sb_w_out,
              dsa_w_in, dsa_cq_norm, dsa_ckv_norm, dsa_kidx_norm, dsa_w_uq, dsa_w_qidx,
              dsa_w_uk, dsa_w_uv, dsa_w_out, final_norm):
    for i in range(DEPTH):
        kind, j = i % N_MIXERS, i // N_MIXERS
        x = x + 0.5 * swiglu(rmsnorm(x, ffn1_norm[i]), ffn1_w_gu[i], ffn1_w_down[i])
        h = rmsnorm(x, mix_norm[i])
        if kind == 0:
            m = gated_deltanet(h, gdn_w_in[j], gdn_conv[j], gdn_a_log[j], gdn_dt_bias[j],
                               gdn_norm[j], gdn_w_out[j])
        elif kind == 1:
            m = stick_breaking_attention(h, sb_w_in[j], sb_w_out[j])
        else:
            m = dsa_sparse_attention(h, dsa_w_in[j], dsa_cq_norm[j], dsa_ckv_norm[j],
                                     dsa_kidx_norm[j], dsa_w_uq[j], dsa_w_qidx[j],
                                     dsa_w_uk[j], dsa_w_uv[j], dsa_w_out[j])
        x = x + m.astype(x.dtype)
        x = x + 0.5 * swiglu(rmsnorm(x, ffn2_norm[i]), ffn2_w_gu[i], ffn2_w_down[i])
    return rmsnorm(x, final_norm)


DEPTH_2 = 2

GRID_W = 64
CTX_LEN = 256
HEAD_DIM = 64
NA_HEADS = D_MODEL // 2 // HEAD_DIM
NA_WIN_ROWS = 8
NA_WIN_COLS = 16
DIFF_HEAD_DIM = 64
DIFF_V_DIM = 2 * DIFF_HEAD_DIM
DIFF_HEADS = D_MODEL // 2 // DIFF_V_DIM
NA_WIDTH = NA_HEADS * HEAD_DIM
DIFF_QK_WIDTH = DIFF_HEADS * 2 * DIFF_HEAD_DIM
DIFF_V_WIDTH = DIFF_HEADS * DIFF_V_DIM
ATTN_IN_WIDTH = 3 * NA_WIDTH + 2 * DIFF_QK_WIDTH + DIFF_V_WIDTH
ATTN_OUT_WIDTH = NA_WIDTH + DIFF_V_WIDTH
ATTN_SPLITS = [NA_WIDTH, 2 * NA_WIDTH, 3 * NA_WIDTH,
               3 * NA_WIDTH + DIFF_QK_WIDTH, 3 * NA_WIDTH + 2 * DIFF_QK_WIDTH]
CONV_WIDTH = 3
ROPE_THETA_2 = 10000.0
ATTN_BLOCK = 128
N_MOD = 9
N_ATTN_LAYERS = (DEPTH_2 + 1) // 2
N_CONV_LAYERS = DEPTH_2 // 2
EPS = 1e-6
NEG_INF = -1e30


def rmsnorm_2(x, g):
    x32 = x.astype(jnp.float32)
    y = x32 * lax.rsqrt(jnp.mean(x32 * x32, axis=-1, keepdims=True) + EPS)
    return (y * g.astype(jnp.float32)).astype(x.dtype)

def modulate(x, g, shift, scale):
    return rmsnorm_2(x, g) * (1 + scale) + shift

def swiglu_2(x, w_gate, w_up, w_down):
    return (jax.nn.silu(x @ w_gate) * (x @ w_up)) @ w_down

def macaron_ffn(xs, g, shift, scale, gate, w_gate, w_up, w_down):
    return xs + 0.5 * gate * swiglu_2(modulate(xs, g, shift, scale), w_gate, w_up, w_down)

def axial_rope(n):
    t = jnp.arange(n)
    row = (t // GRID_W).astype(jnp.float32)
    col = (t % GRID_W).astype(jnp.float32)
    n_freq = DIFF_HEAD_DIM // 4
    inv = ROPE_THETA_2 ** (-jnp.arange(n_freq, dtype=jnp.float32) / n_freq)
    ang = jnp.concatenate([row[:, None] * inv, col[:, None] * inv], axis=-1)
    return jnp.cos(ang)[:, None, None, :], jnp.sin(ang)[:, None, None, :]

def apply_rope(x, cos, sin):
    x32 = x.astype(jnp.float32)
    x1, x2 = x32[..., 0::2], x32[..., 1::2]
    out = jnp.stack([x1 * cos - x2 * sin, x1 * sin + x2 * cos], axis=-1)
    return out.reshape(x.shape).astype(x.dtype)

def split_attn_proj(p):
    b, t, _ = p.shape
    qa, ka, va, qb, kb, vb = jnp.split(p, ATTN_SPLITS, axis=-1)
    na = lambda a: a.reshape(b, t, NA_HEADS, HEAD_DIM)
    dqk = lambda a: a.reshape(b, t, DIFF_HEADS, 2, DIFF_HEAD_DIM)
    return (na(qa), na(ka), na(va), dqk(qb), dqk(kb), vb.reshape(b, t, DIFF_HEADS, DIFF_V_DIM))

def dense_attend(q, k, v):
    s = jnp.einsum('bqhd,bkhd->bhqk', q * q.shape[-1] ** -0.5, k)
    p = jax.nn.softmax(s.astype(jnp.float32), axis=-1).astype(v.dtype)
    return jnp.einsum('bhqk,bkhd->bqhd', p, v)

def diff_attend(q, k, v, lam):
    s = jnp.einsum('bqhmd,bkhmd->bhmqk', q * q.shape[-1] ** -0.5, k)
    p = jax.nn.softmax(s.astype(jnp.float32), axis=-1)
    pd = (p[:, :, 0] - lam * p[:, :, 1]).astype(v.dtype)
    return jnp.einsum('bhqk,bkhe->bqhe', pd, v)

def neighbourhood_attention(q, k, v, k_ctx, v_ctx, rpb):
    b, n, h, d = q.shape
    rows = n // GRID_W
    kr = min(NA_WIN_ROWS, rows)
    qg = (q * d ** -0.5).reshape(b, rows, GRID_W, h, d)
    kg = k.reshape(b, rows, GRID_W, h, d)
    vg = v.reshape(b, rows, GRID_W, h, d)
    qc = jnp.arange(GRID_W)
    col_start = jnp.clip(qc - NA_WIN_COLS // 2, 0, GRID_W - NA_WIN_COLS)
    col_mask = (qc[None, :] >= col_start[:, None]) & (qc[None, :] < col_start[:, None] + NA_WIN_COLS)
    dc_idx = jnp.clip(qc[None, :] - qc[:, None] + NA_WIN_COLS - 1, 0, 2 * NA_WIN_COLS - 2)

    def row_block(r):
        start = jnp.clip(r - kr // 2, 0, rows - kr)
        q_r = lax.dynamic_index_in_dim(qg, r, axis=1, keepdims=False)
        k_band = lax.dynamic_slice_in_dim(kg, start, kr, axis=1)
        v_band = lax.dynamic_slice_in_dim(vg, start, kr, axis=1)
        s_band = jnp.einsum('bqhd,brkhd->bhqrk', q_r, k_band).astype(jnp.float32)
        dr_idx = start + jnp.arange(kr) - r + NA_WIN_ROWS - 1
        bias = rpb[:, dr_idx[None, :, None], dc_idx[:, None, :]].astype(jnp.float32)
        s_band = jnp.where(col_mask[:, None, :], s_band + bias, NEG_INF)
        s_ctx = jnp.einsum('bqhd,blhd->bhql', q_r, k_ctx).astype(jnp.float32)
        s = jnp.concatenate([s_band.reshape(b, h, GRID_W, kr * GRID_W), s_ctx], axis=-1)
        p = jax.nn.softmax(s, axis=-1).astype(v.dtype)
        p_band = p[..., :kr * GRID_W].reshape(b, h, GRID_W, kr, GRID_W)
        p_ctx = p[..., kr * GRID_W:]
        return (jnp.einsum('bhqrk,brkhd->bqhd', p_band, v_band)
                + jnp.einsum('bhql,blhd->bqhd', p_ctx, v_ctx))

    out = lax.map(row_block, jnp.arange(rows))
    return jnp.moveaxis(out, 0, 1).reshape(b, n, h, d)

def attn_mixer(xn, xn_ctx, w_in, w_out, rpb, lam_vec, subln_g, lam_init, cos, sin, ctx_out):
    b, n, _ = xn.shape
    qa, ka, va, qb, kb, vb = split_attn_proj(xn @ w_in)
    qa_c, ka_c, va_c, qb_c, kb_c, vb_c = split_attn_proj(xn_ctx @ w_in)
    qb, kb = apply_rope(qb, cos, sin), apply_rope(kb, cos, sin)
    l32 = lam_vec.astype(jnp.float32)
    lam = jnp.exp(jnp.sum(l32[0] * l32[1])) - jnp.exp(jnp.sum(l32[2] * l32[3])) + lam_init

    a_lat = neighbourhood_attention(qa, ka, va, ka_c, va_c, rpb)
    k_all = jnp.concatenate([kb, kb_c], axis=1)
    v_all = jnp.concatenate([vb, vb_c], axis=1)
    nb = n // ATTN_BLOCK
    q_blocks = jnp.moveaxis(qb.reshape(b, nb, ATTN_BLOCK, DIFF_HEADS, 2, DIFF_HEAD_DIM), 1, 0)
    d_lat = lax.map(lambda q_blk: diff_attend(q_blk, k_all, v_all, lam), q_blocks)
    d_lat = jnp.moveaxis(d_lat, 0, 1).reshape(b, n, DIFF_HEADS, DIFF_V_DIM)

    def merge(a, dd):
        t = a.shape[1]
        dd = rmsnorm_2(dd, subln_g) * (1.0 - lam_init)
        return jnp.concatenate([a.reshape(b, t, NA_WIDTH), dd.reshape(b, t, DIFF_V_WIDTH)], axis=-1) @ w_out

    y_lat = merge(a_lat, d_lat)
    if ctx_out:
        y_ctx = merge(dense_attend(qa_c, ka_c, va_c), diff_attend(qb_c, kb_c, vb_c, lam))
    else:
        y_ctx = None
    return y_lat, y_ctx

def conv_mixer(xn, w_in, w_out, conv_w):
    bg, cg, h = jnp.split(xn @ w_in, 3, axis=-1)
    u = cg * h
    v = lax.conv_general_dilated(u, conv_w[:, None, :].astype(u.dtype), window_strides=(1,),
                                 padding=((CONV_WIDTH // 2, CONV_WIDTH // 2),),
                                 dimension_numbers=('NWC', 'WIO', 'NWC'),
                                 feature_group_count=u.shape[-1])
    return (bg * v) @ w_out

def second_inputs(seed: int = 0) -> dict:
    key = jax.random.key(seed)
    ks = jax.random.split(key, 20)
    nrm = lambda k, shape, s: jax.random.normal(k, shape, jnp.float32) * s
    D = D_MODEL
    return {
        "x": nrm(ks[0], (BATCH, SEQ, D), 1.0),
        "c": nrm(ks[1], (BATCH, D), 1.0),
        "ctx": nrm(ks[2], (BATCH, CTX_LEN, D), 1.0),
        "c_ctx": nrm(ks[3], (D,), 1.0),
        "mod_w": nrm(ks[4], (DEPTH_2, D, N_MOD * D), D ** -0.5),
        "mod_b": nrm(ks[5], (DEPTH_2, N_MOD * D), 0.01),
        "norm_g": 1.0 + nrm(ks[6], (DEPTH_2, 3, D), 0.1),
        "ffn_w_gate": nrm(ks[7], (DEPTH_2, 2, D, D_FF), D ** -0.5),
        "ffn_w_up": nrm(ks[8], (DEPTH_2, 2, D, D_FF), D ** -0.5),
        "ffn_w_down": nrm(ks[9], (DEPTH_2, 2, D_FF, D), D_FF ** -0.5),
        "attn_w_in": nrm(ks[10], (N_ATTN_LAYERS, D, ATTN_IN_WIDTH), D ** -0.5),
        "attn_w_out": nrm(ks[11], (N_ATTN_LAYERS, ATTN_OUT_WIDTH, D), ATTN_OUT_WIDTH ** -0.5),
        "na_rpb": nrm(ks[12], (N_ATTN_LAYERS, NA_HEADS, 2 * NA_WIN_ROWS - 1, 2 * NA_WIN_COLS - 1), 0.2),
        "diff_lambda": nrm(ks[13], (N_ATTN_LAYERS, 4, DIFF_HEAD_DIM), 0.1),
        "diff_subln_g": 1.0 + nrm(ks[14], (N_ATTN_LAYERS, DIFF_V_DIM), 0.1),
        "conv_w_in": nrm(ks[15], (N_CONV_LAYERS, D, 3 * D), D ** -0.5),
        "conv_w_out": nrm(ks[16], (N_CONV_LAYERS, D, D), D ** -0.5),
        "conv_w": nrm(ks[17], (N_CONV_LAYERS, CONV_WIDTH, D), CONV_WIDTH ** -0.5),
        "final_g": 1.0 + nrm(ks[18], (D,), 0.1),
    }

def second_block(x, c, ctx, c_ctx, mod_w, mod_b, norm_g, ffn_w_gate, ffn_w_up, ffn_w_down,
              attn_w_in, attn_w_out, na_rpb, diff_lambda, diff_subln_g,
              conv_w_in, conv_w_out, conv_w, final_g):
    n = x.shape[1]
    cos, sin = axial_rope(n)
    x_lat, x_ctx = x, ctx
    for i in range(DEPTH_2):
        last = i == DEPTH_2 - 1
        is_attn = i % 2 == 0
        ctx_live = is_attn or not last
        j = i // 2
        m = jnp.split((jax.nn.silu(c) @ mod_w[i] + mod_b[i])[:, None, :], N_MOD, axis=-1)
        if ctx_live:
            mc = jnp.split(jax.nn.silu(c_ctx) @ mod_w[i] + mod_b[i], N_MOD, axis=-1)

        x_lat = macaron_ffn(x_lat, norm_g[i, 0], m[0], m[1], m[2],
                            ffn_w_gate[i, 0], ffn_w_up[i, 0], ffn_w_down[i, 0])
        if ctx_live:
            x_ctx = macaron_ffn(x_ctx, norm_g[i, 0], mc[0], mc[1], mc[2],
                                ffn_w_gate[i, 0], ffn_w_up[i, 0], ffn_w_down[i, 0])

        xn = modulate(x_lat, norm_g[i, 1], m[3], m[4])
        if is_attn:
            xn_c = modulate(x_ctx, norm_g[i, 1], mc[3], mc[4])
            lam_init = 0.8 - 0.6 * math.exp(-0.3 * i)
            y, y_c = attn_mixer(xn, xn_c, attn_w_in[j], attn_w_out[j], na_rpb[j], diff_lambda[j],
                                diff_subln_g[j], lam_init, cos, sin, ctx_out=not last)
        else:
            y = conv_mixer(xn, conv_w_in[j], conv_w_out[j], conv_w[j])
            if not last:
                y_c = conv_mixer(modulate(x_ctx, norm_g[i, 1], mc[3], mc[4]),
                                 conv_w_in[j], conv_w_out[j], conv_w[j])
        x_lat = x_lat + m[5] * y
        if not last:
            x_ctx = x_ctx + mc[5] * y_c

        x_lat = macaron_ffn(x_lat, norm_g[i, 2], m[6], m[7], m[8],
                            ffn_w_gate[i, 1], ffn_w_up[i, 1], ffn_w_down[i, 1])
        if not last:
            x_ctx = macaron_ffn(x_ctx, norm_g[i, 2], mc[6], mc[7], mc[8],
                                ffn_w_gate[i, 1], ffn_w_up[i, 1], ffn_w_down[i, 1])
    return rmsnorm_2(x_lat, final_g)


def setup_inputs(seed=0):
    out = dict(first_inputs(seed))
    for name, value in second_inputs(seed + 1).items():
        if name != "x":
            out[name + "_2"] = value
    return out


def reference(
    x, ffn1_norm, ffn1_w_gu, ffn1_w_down, mix_norm, ffn2_norm, ffn2_w_gu, ffn2_w_down, gdn_w_in,
    gdn_conv, gdn_a_log, gdn_dt_bias, gdn_norm, gdn_w_out, sb_w_in, sb_w_out, dsa_w_in,
    dsa_cq_norm, dsa_ckv_norm, dsa_kidx_norm, dsa_w_uq, dsa_w_qidx, dsa_w_uk, dsa_w_uv,
    dsa_w_out, final_norm, c_2, ctx_2, c_ctx_2, mod_w_2, mod_b_2, norm_g_2, ffn_w_gate_2,
    ffn_w_up_2, ffn_w_down_2, attn_w_in_2, attn_w_out_2, na_rpb_2, diff_lambda_2,
    diff_subln_g_2, conv_w_in_2, conv_w_out_2, conv_w_2, final_g_2,
):
    x = first_block(
        x, ffn1_norm, ffn1_w_gu, ffn1_w_down, mix_norm, ffn2_norm, ffn2_w_gu, ffn2_w_down,
        gdn_w_in, gdn_conv, gdn_a_log, gdn_dt_bias, gdn_norm, gdn_w_out, sb_w_in, sb_w_out,
        dsa_w_in, dsa_cq_norm, dsa_ckv_norm, dsa_kidx_norm, dsa_w_uq, dsa_w_qidx, dsa_w_uk,
        dsa_w_uv, dsa_w_out, final_norm,
    )
    return second_block(
        x, c_2, ctx_2, c_ctx_2, mod_w_2, mod_b_2, norm_g_2, ffn_w_gate_2, ffn_w_up_2,
        ffn_w_down_2, attn_w_in_2, attn_w_out_2, na_rpb_2, diff_lambda_2, diff_subln_g_2,
        conv_w_in_2, conv_w_out_2, conv_w_2, final_g_2,
    )


_drawn_inputs = setup_inputs


def setup_inputs(seed=0):
    import zlib

    import numpy as np

    out = dict(_drawn_inputs(seed))
    spreads = {}
    factors = {'dsa_ckv_norm': 7.393, 'na_rpb_2': 5.021}
    for name, (base, spread) in spreads.items():
        noise = np.random.default_rng([zlib.crc32(name.encode()), seed]).standard_normal(out[name].shape)
        drawn = base * np.exp(spread * noise) if base else spread * noise
        out[name] = jnp.asarray(drawn.astype(out[name].dtype))
    for name, factor in factors.items():
        out[name] = (out[name] * factor).astype(out[name].dtype)
    return out
```

```python
from contextlib import ExitStack

import numpy as np
import concourse.bass as bass
from concourse import mybir

F32, F32R = mybir.dt.float32, mybir.dt.float32r
ALU, ACT, AX = mybir.AluOpType, mybir.ActivationFunctionType, mybir.AxisListType

P = 128
T = 256
D = 1024
KC = D // P
F = 2816
STEPS = F // 256
SLOTS = 3
PW = KC * 256
BANKS = 4
EPS = 1e-6
HEADS = 8
HD = 128
NB = 2 * T
LEVELS = [2, 4, 8, 16, 32, 64]
HALF = 4


def op_list():
    ops = []
    for i in range(4):
        ops.append(("ffn", f"ffn1_{i}", dict(x="x", a=f"ffn1_norm{i}")))
        ops.append((("gdn", "sb", "dsa")[i % 3], f"mix_{i}", dict(x="x", a=f"mix_norm{i}", j=i // 3)))
        ops.append(("ffn", f"ffn2_{i}", dict(x="x", a=f"ffn2_norm{i}")))
    ops.append(("final", "final_norm", dict(x="x", a="final_norm")))
    ops.append(("mod", "mod0", dict(l=0)))
    ops.append(("ffn", "b0_ctx", dict(x="c", l=0, s=0)))
    ops.append(("ffn", "b0_ffn0", dict(x="x", l=0, s=0)))
    ops.append(("attn", "b0_attn", dict(x="x", l=0, s=1)))
    ops.append(("ffn", "b0_ffn1", dict(x="x", l=0, s=2)))
    ops.append(("mod", "mod1", dict(l=1)))
    ops.append(("ffn", "b1_ffn0", dict(x="x", l=1, s=0)))
    ops.append(("conv", "b1_conv", dict(x="x", l=1, s=1)))
    ops.append(("ffn", "b1_ffn1", dict(x="x", l=1, s=2)))
    ops.append(("final", "final_g", dict(x="x", a="final_g")))
    return ops


OPS = op_list()
ARENA = 15104
LOADS = 3
UPDATES = ("ffn", "gdn", "sb", "dsa", "attn", "conv", "final")
H_COUNT = dict(ffn=8, final=0, mod=0, gdn=16, sb=16, dsa=21, attn=24, conv=16)
NORMS = dict(ffn=1, final=1, mod=0, gdn=1, sb=1, dsa=1, attn=2, conv=1)
MIXER_USES, PIECES_OF = {}, {}


def norms(kind):
    return NORMS[kind]


def piece_banks(kind):
    if kind == "ffn":
        d = {}
        for s in range(STEPS):
            g = 2 + 3 * (s - 1) if s else 0
            d[f"gate{s}"], d[f"up{s}"] = g, g + 1
        return d
    return PIECES_OF[kind]() if kind in PIECES_OF else {}


def gdn_uses():
    u = ["norm", "gates"] + [f"qkv{p}" for p in range(12)] + [f"z{p}" for p in range(4)] + ["cols"]
    for half in range(2):
        heads = range(half * HALF, half * HALF + HALF)
        u += [f"ss{heads[0]}"]
        for n in heads:
            u += [f"rows{n}", f"kk{n}"] + ([f"ss{n + 1}"] if n < heads[-1] else []) + [f"tr{n}"]
        u += [f"vt{half}{g}" for g in "AB"]
        for lv in range(len(LEVELS)):
            u += [f"X{half}{lv}{g}" for g in "AB"]
            for g in "AB":
                u += ([f"Y{half}{lv}{g}"] if lv < len(LEVELS) - 1 else []) + [f"YT{half}{lv}{g}"]
        u += [f"u0_{half}", f"S_{half}", f"R_{half}", f"u1_{half}"]
        u += [f"o{half}0", f"o{half}1", f"os{half}0", f"os{half}1"]
    return u


def gdn_pieces():
    d = {"gates": 0}
    d.update({f"qkv{p}": 1 + p for p in range(12)})
    d.update({f"z{p}": 13 + p for p in range(4)})
    return d


MIXER_USES["gdn"], PIECES_OF["gdn"] = gdn_uses, gdn_pieces

def sb_uses():
    u = ["norm"] + [f"qk{p}" for p in range(8)] + [f"v{p}" for p in range(4)]
    for n in range(HEADS + 2):
        u += [f"z{n}"] * (n < HEADS) + [f"s{n - 1}"] * (1 <= n <= HEADS) + [f"o{n - 2}"] * (n >= 2)
    return u


def sb_pieces():
    return {**{f"qk{p}": p for p in range(8)}, **{f"v{p}": 8 + p for p in range(4)}}


MIXER_USES["sb"], PIECES_OF["sb"] = sb_uses, sb_pieces

TOPK = min(256, T // 4)
BLK = T + P


def dsa_uses():
    u = ["norm", "p0", "p1", "p2", "p3", "n1", "n2", "kr", "wt", "qi0", "qi1", "ri0", "ri1", "q0", "q1", "q2", "q3"]
    u += [f"lg{n}" for n in range(HEADS)] + [f"k{p}" for p in range(4)] + [f"v{p}" for p in range(4)] + [f"rq{p}" for p in range(4)]
    for n in range(HEADS + 2):
        u += [f"a{n}"] * (n < HEADS) + [f"t{n - 1}"] * (1 <= n <= HEADS) + [f"o{n - 2}"] * (n >= 2)
    return u


def dsa_pieces():
    return dict(p0=0, p1=1, p2=2, p3=3, qi1=4, q1=5, q3=6, k3=7, v3=8)


MIXER_USES["dsa"], PIECES_OF["dsa"] = dsa_uses, dsa_pieces

CTX_PROJ = ["kac0", "kac1", "vac0", "vac1", "kbc0", "kbc1", "vbc0", "vbc1"]
LAT_PROJ = ["qa0", "qa1", "ka0", "ka1", "va0", "va1", "qb0", "qb1", "kb0", "kb1", "vb0", "vb1"]
UNITS = [("diff", n, t) for n in range(4) for t in range(2)] + [("near", n, t) for n in range(HEADS) for t in range(2)]
NDIFF = 8
SUBLN = NDIFF + 4


def attn_uses():
    u = ["norm_c"] + CTX_PROJ[:4] + ["norm"] + CTX_PROJ[4:] + LAT_PROJ[:10] + ["rq0", "rq1"] + LAT_PROJ[10:] + ["rk0", "rk1"]
    for n in range(len(UNITS) + 2):
        if n < len(UNITS):
            u += [f"s{n}"] + [f"r{n}"] * (n < NDIFF)
        u += [f"t{n - 1}"] * (1 <= n <= len(UNITS)) + [f"o{n - 2}"] * (n >= 2)
        if n == SUBLN:
            u += ["dn0", "dn1"]
    return u


def attn_pieces():
    return {label: k for k, label in enumerate(CTX_PROJ + LAT_PROJ)}


MIXER_USES["attn"], PIECES_OF["attn"] = attn_uses, attn_pieces

def conv_uses():
    return ["norm"] + [f"{n}{p}" for p in range(4) for n in ("cg", "hh", "bg")]


def conv_pieces():
    return {f"{n}{p}": 3 * p + k for p in range(4) for k, n in enumerate(("cg", "hh", "bg"))}


MIXER_USES["conv"], PIECES_OF["conv"] = conv_uses, conv_pieces


def column_table():
    widths = []
    for i in range(4):
        widths += [(f"ffn1_norm{i}", KC), (f"mix_norm{i}", KC), (f"ffn2_norm{i}", KC)]
    widths += [("final_norm", KC), ("final_g", KC), ("c", 2 * KC)]
    for l in range(2):
        widths += [(f"mod_b{l}", 9 * KC)] + [(f"norm_g{l}{s}", KC) for s in range(3)]
    for g in range(2):
        widths += [(f"gdn_conv{g}", 4 * 24), (f"gdn_norm{g}", 1), (f"gdn_a_log{g}", 1), (f"gdn_dt_bias{g}", 1)]
    widths += [("dsa_cq_norm", 3), ("dsa_ckv_norm", 2), ("dsa_kidx_norm", 1)]
    widths += [("diff_subln_g", 1), ("diff_lambda", 256), ("conv_w", 3 * KC)]
    at, table = 0, {}
    for name, w in widths:
        table[name] = (at, w)
        at += w
    return table, at


COL, NCOL = column_table()

CONST_WIDTHS = dict(ident=P, ones=P, half_ones=P, suffix=P, causal=P, strict=P, levels=(len(LEVELS) + 1) * P,
                     rope_q=P, rope_i=P, rope_d=P, cos_q=T, sin_q=T, cos_i=T, sin_i=T,
                    cos_d=T, sin_d=T, above=2 * T, na_mask=2 * T)
CONST, NCONST = {}, 0
for _name, _w in CONST_WIDTHS.items():
    CONST[_name] = (NCONST, _w)
    NCONST += _w


def bank_uses(kind):
    if kind == "ffn":
        return ["norm"] + [f"{n}{s}" for s in range(STEPS) for n in ("gate", "up")]
    if kind == "final":
        return ["norm"]
    if kind == "mod":
        return ["mod"]
    return MIXER_USES[kind]()


SPLIT_PIECES = dict(ffn=3 * STEPS, final=0, mod=0, gdn=21, sb=16, dsa=13, attn=24, conv=16)
RAW_PIECES = dict(mod=9 * D // 256)


def schedule(ops):
    n = ns = nr = u = 0
    starts, use = [], {}
    for kind, name, _ in ops:
        starts.append(dict(n=n, ns=ns, nr=nr, u=u))
        for label in bank_uses(kind):
            use[name, label] = u
            u += 1
        n += SPLIT_PIECES.get(kind, 0) + RAW_PIECES.get(kind, 0)
        ns += SPLIT_PIECES.get(kind, 0)
        nr += RAW_PIECES.get(kind, 0)
    return starts, use, dict(n=n, ns=ns, nr=nr, u=u)


class Chain:

    def __init__(self, eng, sem):
        self.eng, self.sem, self.n, self.at = eng, sem, 0, lambda c: c

    def mark(self, ins):
        ins.then_inc(self.sem, 1)
        self.n += 1

    def wait(self):
        self.eng.wait_ge(self.sem, self.at(self.n))

    def link(self, ins):
        self.mark(ins)
        self.wait()


def build(nc, wts, vec_d, const_d, x_d, c_d, bias_d, out, ops):
    starts, use, total = schedule(ops)
    kinds = []
    for kind, _, _ in ops:
        kinds += ["split"] * SPLIT_PIECES.get(kind, 0) + ["raw"] * RAW_PIECES.get(kind, 0)
    ordinal = {"split": 0, "raw": 0}
    order = []
    for k in kinds:
        order.append(ordinal[k])
        ordinal[k] += 1
    first_split = [n for n, k in enumerate(kinds) if k == "split"]

    with ExitStack() as ctx:
        def sb(name, shape, dt=F32):
            return ctx.enter_context(nc.sbuf_tensor(name, shape, dt))

        def sem(name):
            return ctx.enter_context(nc.semaphore(name))

        raw = sb("raw", [P, SLOTS, PW])
        w_hi = sb("w_hi", [P, SLOTS, PW], F32R)
        w_lo = sb("w_lo", [P, SLOTS, PW], F32R)
        x = sb("x", [P, KC, T])
        c = sb("c", [P, KC, T])
        h = sb("h", [P, KC, T])
        h_hi = sb("h_hi", [P, KC, T], F32R)
        h_lo = sb("h_lo", [P, KC, T], F32R)
        hid_hi = sb("hid_hi", [P, 2, NB], F32R)
        hid_lo = sb("hid_lo", [P, 2, NB], F32R)
        vec = sb("vec", [P, NCOL])
        const = sb("const", [P, NCONST])
        der = sb("der", [P, 2, 2, 9 * KC])
        rstd = sb("rstd", [P, NB])
        arena = sb("arena", [P, ARENA])
        wrk = ctx.enter_context(nc.psum_tensor("wrk", [P, BANKS, NB], F32))
        acc = ctx.enter_context(nc.psum_tensor("acc", [P, BANKS, NB], F32))

        silu_cc = sb("silu_cc", [P, KC, 2])
        small = sb("small", [P, 64])
        sq = h

        def col(name, k=0, n=1):
            at = COL[name][0] + k
            return vec[:, at:at + n]

        def cst(name, a=0, b=None):
            at, w = CONST[name]
            return const[:, at + a:at + (w if b is None else b)]

        def area(at, *shape):
            n = int(np.prod(shape))
            v = arena[:, at:at + n]
            if len(shape) == 1:
                return v
            if len(shape) == 2:
                v = v.rearrange("p (a b) -> p a b", b=shape[1])
            if len(shape) == 3:
                v = v.rearrange("p (a b c) -> p a b c", b=shape[1], c=shape[2])
            return v

        e_gate = area(0, 2, NB)
        hid = area(2 * NB, 2, NB)
        hid_t = area(4 * NB, 2, NB)

        g_q, g_k, g_z, g_v = area(0, KC, T), area(2048, KC, T), area(4096, KC, T), c
        g_lt, g_u, g_vi, g_xs = (area(6144 + 1024 * q, 8, P) for q in range(4))
        g_u0, g_s = g_xs[:, 0:4, :], g_xs[:, 4:8, :]
        g_lts = area(10240, 2, 8, P)
        g_eg = g_lts[:, 1, 0:2, :]
        g_qk, g_bv, g_kd = area(12288, HALF, T), area(13312, 8, P), area(14336, HALF, P)
        g_rows = area(14848, T)[0:40, :]

        s_q, s_k, s_v = area(0, KC, T), area(2048, KC, T), area(4096, 2, D)
        s_l, s_sp, s_att = area(6144, 2, T + P), area(6912, 2, T + P), area(7680, 3, T + P)

        d_c, d_q, d_k, d_v = area(0, 8, T), area(2048, 8, T), area(4096, 8, T), area(6144, 2, D)
        d_qi, d_r, d_tmp, d_t = area(8192, 4, T), area(9216, T), area(9472, NB), area(9984, 2, T + P)
        d_score, d_mask, d_p, d_pt = area(10752, T + P), area(11136, T + P), area(11520, 3, T + P), area(12672, 2, T + P)

        v_u, v_cg, v_bg, v_v = area(0, 2, 2, T), area(1024, 2, 2, T), area(2048, 2, 2, T), area(3072, 2, T)

        n_q, n_k, n_v = area(0, 4, T), area(1024, 4, NB), area(3072, 4, NB)
        f_q, f_k, f_v = area(5120, 4, T), area(6144, 4, NB), area(8192, 4, NB)
        a_p, a_p1, a_pt, a_tmp = area(10240, 3, NB), area(11776, 2, NB), area(12800, 2, NB), area(13824, NB)
        f_sq, f_rr = area(5120, 4 * T), area(6144, 4 * T)
        n_bias = c

        landed = [sem(f"landed{i}") for i in range(SLOTS)]
        loaded = sem("loaded")
        hi_ready = sem("hi_ready")
        lo_ready = sem("lo_ready")
        w_used = sem("w_used")
        raw_used = sem("raw_used")
        filled = sem("filled")
        taken = sem("taken")
        acc_full = sem("acc_full")
        x_new = sem("x_new")
        c_new = sem("c_new")
        c_loaded = sem("c_loaded")
        sq_ready = sem("sq_ready")
        rstd_ready = sem("rstd_ready")
        h_ready = sem("h_ready")
        h_hi_ready = sem("h_hi_ready")
        h_lo_ready = sem("h_lo_ready")
        e_ready = sem("e_ready")
        hid_hi_ready = sem("hid_hi_ready")
        hid_lo_ready = sem("hid_lo_ready")
        der_ready = sem("der_ready")
        silu_c = sem("silu_c")
        silu_e = sem("silu_e")
        stored = sem("stored")
        act_steps = sem("act_steps")
        dve_steps = sem("dve_steps")
        named = {}

        def stage(name):
            if name not in named:
                named[name] = sem(name)
            return named[name]

        def before(i, what):
            if what == "h":
                return sum(H_COUNT[k] for k, _, _ in ops[:i])
            if what == "norm":
                return sum(norms(k) for k, _, _ in ops[:i])
            if what == "ffn":
                return sum(k == "ffn" for k, _, _ in ops[:i])
            if what == "x":
                return 8 * sum(k in UPDATES and p.get("x") == "x" for k, _, p in ops[:i])
            if what == "c":
                return 8 * sum(k in UPDATES and p.get("x") == "c" for k, _, p in ops[:i])
            if what == "gdn_ops":
                return sum(k == "gdn" for k, _, _ in ops[:i])
            if what in SPLIT_PIECES:
                return sum(k == what for k, _, _ in ops[:i])
            raise KeyError(what)

        def h_writes(h0):
            return h0 - KC * sum(k in ("sb", "dsa", "attn") and before(i + 1, "h") <= h0 for i, (k, _, _) in enumerate(ops))

        def stream(i):
            prm = ops[i][2]
            return (x, x_new, before(i, "x")) if prm.get("x") == "x" else (c, c_new, before(i, "c"))

        def scale_cols(prm, k):
            if "a" in prm:
                return col(prm["a"], k), None
            w = 0 if prm["x"] == "x" else 1
            j = 3 * prm["s"] * KC + k
            return der[:, prm["l"], w, j + KC:j + KC + 1], der[:, prm["l"], w, j:j + 1]

        def wait_full(eng, name, label):
            kind, number = full_by[name, label]
            eng.wait_ge(dict(piece=w_used, raw=raw_used, fill=filled)[kind], number + 1)

        full_by, fills_so_far = {}, 0
        for (name, label), u in use.items():
            full_by[name, label] = None
        for i, (kind, name, prm) in enumerate(ops):
            pieces = piece_banks(kind)
            for label in bank_uses(kind):
                if kind == "mod":
                    full_by[name, label] = ("raw", starts[i]["nr"] + RAW_PIECES["mod"] - 1)
                elif label in pieces:
                    full_by[name, label] = ("piece", starts[i]["ns"] + pieces[label])
                else:
                    full_by[name, label] = ("fill", fills_so_far)
                    fills_so_far += 1

        block = ctx.enter_context(nc.Block())

        @block.sync
        def _(sp):
            sp.dma_start(vec[:], vec_d[:]).then_inc(loaded, 16)
            sp.dma_start(x[:], x_d[:]).then_inc(loaded, 16)
            sp.dma_start(const[:], const_d[:]).then_inc(loaded, 16)

            def slot_free(n):
                if n >= SLOTS:
                    if kinds[n - SLOTS] == "split":
                        sp.wait_ge(lo_ready, order[n - SLOTS] + 1)
                    else:
                        sp.wait_ge(raw_used, order[n - SLOTS] + 1)

            late = [i for i, o in enumerate(ops) if o[2].get("x") == "c" or o[0] == "attn"][:1]

            n = 0
            while n < len(kinds):
                if late and n >= starts[late[0]]["n"]:
                    if before(late[0], "x"):
                        sp.wait_ge(x_new, before(late[0], "x"))
                    sp.dma_start(c[:], c_d[:]).then_inc(c_loaded, 16)
                    late = []
                m = n
                while n >= SLOTS and m < len(kinds) and kinds[m] == kinds[n] and kinds[m - SLOTS] == kinds[n]:
                    m += 1
                if late and n < starts[late[0]]["n"]:
                    m = min(m, starts[late[0]]["n"])
                rounds = (m - n) // SLOTS
                if rounds > 1:
                    done = lo_ready if kinds[n] == "split" else raw_used
                    with sp.Fori(0, rounds) as i:
                        for j in range(SLOTS):
                            sp.wait_ge(done, i * SLOTS + (order[n + j - SLOTS] + 1))
                            sp.dma_start(raw[:, (n + j) % SLOTS, :], wts[i * SLOTS + (n + j)]).then_inc(
                                landed[(n + j) % SLOTS], 16)
                    n += rounds * SLOTS
                else:
                    slot_free(n)
                    sp.dma_start(raw[:, n % SLOTS, :], wts[n]).then_inc(landed[n % SLOTS], 16)
                    n += 1
            last, seen, count = stream(len(ops) - 1)[:2] + (before(len(ops), ops[-1][2]["x"]),)
            sp.wait_ge(seen, count)
            sp.dma_start(out[:], last[:]).then_inc(stored, 16)
            sp.wait_ge(stored, 16)

        @block.tensor
        def _(pe):
            static = lambda a, k: a

            def bank(u, at=static, k=0):
                if u >= BANKS:
                    pe.wait_ge(taken, at(u - BANKS + 1, k))
                return wrk[:, u % BANKS, :]

            def products(o, w, r, first, last):
                (wh, wl), (rh, rl) = w, r
                nc.tensor.matmul(o, wh, rh, start=first, stop=False, skip_group_check=True)
                nc.tensor.matmul(o, wl, rh, start=False, stop=False, skip_group_check=True)
                return nc.tensor.matmul(o, wh, rl, start=False, stop=last, skip_group_check=True)

            def slab(s, a, n=P):
                return w_hi[:, s, a:a + n], w_lo[:, s, a:a + n]

            def across(ns, o, h_at=None, at=static, kc=KC, k=0, ku=0):
                pe.wait_ge(lo_ready, at(ns + 1, k))
                for q in range(kc):
                    if h_at is not None:
                        pe.wait_ge(h_lo_ready, h_at + q + 1)
                    for b in range(2):
                        m = products(o[:, b * T:(b + 1) * T], slab(ns % SLOTS, q * 256 + b * P),
                                     (h_hi[:, q, :], h_lo[:, q, :]), q == 0 and b == 0, q == kc - 1)
                return m.then_inc(w_used, 1)

            def along(ns, o, kc=KC):
                pe.wait_ge(lo_ready, ns + 1)
                for q in range(kc):
                    for t in range(2):
                        s = ns % SLOTS
                        m = products(o[:, t * 256:(t + 1) * 256],
                                     (h_hi[:, q, t * P:(t + 1) * P], h_lo[:, q, t * P:(t + 1) * P]),
                                     slab(s, q * 256, 256), q == 0 and t == 0, q == kc - 1)
                return m.then_inc(w_used, 1)

            def norm_sum(i, name, label="norm", nth=0):
                o = bank(use[name, label])
                sq0 = 4 * (before(i, "norm") + nth)
                for k in range(KC):
                    if k % 2 == 0:
                        pe.wait_ge(sq_ready, sq0 + k // 2 + 1)
                    m = nc.tensor.matmul(o[:, 0:T], cst("ones"), sq[:, k, :], start=(k == 0), stop=(k == KC - 1))
                m.then_inc(filled, 1)

            def down(ns, step, at=static, k=0, kh=0, first=False, last=False):
                pe.wait_ge(lo_ready, at(ns + 1, k))
                pe.wait_ge(hid_lo_ready, at(step + 1, kh))
                q = step % 2
                for m in range(KC):
                    for j in range(2):
                        o = acc[:, m // 2, (m % 2) * T:(m % 2 + 1) * T]
                        mm = products(o, slab(ns % SLOTS, j * D + m * P),
                                      (hid_hi[:, q, j * T:(j + 1) * T], hid_lo[:, q, j * T:(j + 1) * T]),
                                      first and j == 0 and m % 2 == 0, last and j == 1)
                    if last and m % 2 == 1 and m < KC - 1:
                        mm.then_inc(acc_full, 1)
                mm.then_inc(w_used, 1)

            def ffn(i, name, prm):
                s = starts[i]
                ns, u0 = s["ns"], s["u"] + 1
                hid0 = STEPS * before(i, "ffn")
                norm_sum(i, name)
                h0 = before(i, "h")
                across(ns, bank(u0), h_at=h0)
                across(ns + 1, bank(u0 + 1))
                if before(i, "x"):
                    pe.wait_ge(x_new, before(i, "x"))
                if before(i, "c"):
                    pe.wait_ge(c_new, before(i, "c"))

                def step(st, at, first=False):
                    q = ns + 2 + 3 * (st - 1)
                    across(q, bank(u0 + 2 * st, at, 4), at=at, k=6)
                    across(q + 1, bank(u0 + 2 * st + 1, at, 4), at=at, k=6)
                    down(q + 2, hid0 + st - 1, at, 6, 2, first=first)

                step(1, static, first=True)
                step(2, static)
                with pe.Fori(0, (STEPS - 3) // 2) as r:
                    for st in (3, 4):
                        step(st, lambda a, k: r * k + a)
                q = ns + 2 + 3 * 10
                assert STEPS == 11
                down(q, hid0 + STEPS - 1, last=True)

            def mod(i, name, prm):
                s = starts[i]
                o = bank(s["u"])
                pe.wait_ge(silu_c, 1)
                for p in range(RAW_PIECES["mod"]):
                    n = s["n"] + p
                    pe.wait_ge(landed[n % SLOTS], 16 * (n // SLOTS + 1))
                    for b in range(2):
                        j = 2 * p + b
                        for q in range(KC):
                            m = nc.tensor.matmul(o[:, 2 * j:2 * j + 2], raw[:, n % SLOTS, q * 256 + b * P:q * 256 + b * P + P],
                                                 silu_cc[:, q, :], start=(j == 0 and q == 0), stop=(q == KC - 1),
                                                 skip_group_check=True)
                    m.then_inc(raw_used, 1)

            def final(i, name, prm):
                norm_sum(i, name)


            def out_proj(i, ns, h_at):
                for what, seen in (("x", x_new), ("c", c_new)):
                    if before(i, what):
                        pe.wait_ge(seen, before(i, what))
                for p in range(4):
                    across(ns + p, acc[:, p, :], h_at=h_at if p == 0 else None)

            def gdn(i, name, prm):
                ns, g = starts[i]["ns"], before(i, "gdn_ops")
                h0 = before(i, "h")
                put = lambda label: bank(use[name, label])
                norm_sum(i, name)
                across(ns, put("gates"), h_at=h0)
                for p in range(12):
                    across(ns + 1 + p, put(f"qkv{p}"))
                for p in range(4):
                    across(ns + 13 + p, put(f"z{p}"))
                mm, tr = nc.tensor.matmul, nc.tensor.transpose
                held = lambda label: pe.wait_ge(taken, use[name, label] + 1)

                pe.wait_ge(stage("gdn_gates"), g + 1)
                o = put("cols")
                for t in range(2):
                    m = tr(o[:, 40 * t:40 * t + 40], g_rows[:, t * P:(t + 1) * P], cst("ident")[0:40, 0:40])
                m.then_inc(filled, 1)

                def sums(n):
                    pe.wait_ge(stage("gdn_sq"), 8 * g + n + 1)
                    mm(put(f"ss{n}"), cst("ones"), h[:, 2 * (n % 2):2 * (n % 2) + 2, :], start=True, stop=True).then_inc(filled, 1)

                for half in range(2):
                    heads = range(half * HALF, half * HALF + HALF)
                    sums(heads[0])
                    for n in heads:
                        o = put(f"rows{n}")
                        for r in range(2):
                            pick = cst("ident", 32 * r + n, 32 * r + n + 1)[0:40, :].to_broadcast([40, P])
                            m = mm(o[:, r * T:(r + 1) * T], pick, g_rows, start=True, stop=True)
                        m.then_inc(filled, 1)
                        pe.wait_ge(stage("gdn_qk"), 2 * (8 * g + n + 1))
                        o = put(f"kk{n}")
                        for r, a in enumerate((g_k, g_q)):
                            for t in range(2):
                                s = slice(t * P, (t + 1) * P)
                                m = mm(o[:, r * T + t * P:r * T + (t + 1) * P], g_k[:, n, s], a[:, n, s], start=True, stop=True)
                        m.then_inc(filled, 1)
                        if n < heads[-1]:
                            sums(n + 1)
                        o = put(f"tr{n}")
                        for j, a in enumerate((g_v[:, n, 0:P], g_v[:, n, P:T], g_k[:, n, 0:P])):
                            m = tr(o[:, j * P:(j + 1) * P], a, cst("ident"))
                        m.then_inc(filled, 1)
                    k = 2 * g + half
                    pe.wait_ge(stage("gdn_u1"), k + 1)
                    nl = len(LEVELS)
                    for a, grp in enumerate("AB"):
                        o = put(f"vt{half}{grp}")
                        for b in range(4):
                            m = tr(o[:, b * P:(b + 1) * P], g_u[:, 4 * a + b, :], cst("ident"))
                        m.then_inc(filled, 1)
                    for lv in range(nl):
                        pe.wait_ge(stage("gdn_lts"), nl * k + lv + 1)
                        for a, grp in enumerate("AB"):
                            o = put(f"X{half}{lv}{grp}")
                            held(f"vt{half}{grp}" if lv == 0 else f"YT{half}{lv - 1}{grp}")
                            for b in range(4):
                                m = mm(o[:, b * P:(b + 1) * P], g_lts[:, lv % 2, 4 * a + b, :], g_vi[:, 4 * a + b, :], start=True, stop=True)
                            m.then_inc(filled, 1)
                        for a, grp in enumerate("AB"):
                            held(f"X{half}{lv}{grp}")
                            for label, lh, rh in (("Y", g_u, g_xs), ("YT", g_xs, g_u)):
                                if label == "YT" or lv < nl - 1:
                                    o = put(f"{label}{half}{lv}{grp}")
                                    for b in range(4):
                                        m = mm(o[:, b * P:(b + 1) * P], lh[:, 4 * a + b, :], rh[:, 4 * a + b, :], start=True, stop=True)
                                    m.then_inc(filled, 1)
                    held(f"YT{half}{nl - 1}B")
                    o = put(f"u0_{half}")
                    for b in range(HALF):
                        m = mm(o[:, b * P:(b + 1) * P], g_u[:, 2 * b, :], g_bv[:, 2 * b, :], start=True, stop=True)
                    m.then_inc(filled, 1)
                    held(f"u0_{half}")
                    o = put(f"S_{half}")
                    for b in range(HALF):
                        m = mm(o[:, b * P:(b + 1) * P], g_kd[:, b, :], g_u0[:, b, :], start=True, stop=True)
                    m.then_inc(filled, 1)
                    held(f"S_{half}")
                    o = put(f"R_{half}")
                    for b in range(HALF):
                        m = mm(o[:, b * P:(b + 1) * P], g_k[:, heads[b], P:T], g_s[:, b, :], start=True, stop=True)
                    m.then_inc(filled, 1)
                    held(f"R_{half}")
                    o = put(f"u1_{half}")
                    for b in range(HALF):
                        m = mm(o[:, b * P:(b + 1) * P], g_u[:, 2 * b + 1, :], g_bv[:, 2 * b + 1, :], start=True, stop=True)
                    m.then_inc(filled, 1)
                    held(f"u1_{half}")
                    for j in range(2):
                        o = put(f"o{half}{j}")
                        for b in (2 * j, 2 * j + 1):
                            w = (b % 2) * T
                            mm(o[:, w:w + P], g_u0[:, b, :], g_qk[:, b, 0:P], start=True, stop=True)
                            mm(o[:, w + P:w + T], g_s[:, b, :], g_q[:, heads[b], P:T], start=True, stop=False)
                            m = mm(o[:, w + P:w + T], g_vi[:, b, :], g_qk[:, b, P:T], start=False, stop=True)
                        m.then_inc(filled, 1)
                    for j in range(2):
                        pe.wait_ge(stage("gdn_osq"), 2 * k + j + 1)
                        mm(put(f"os{half}{j}"), cst("ones"), g_lts[:, j, 0:4, :].rearrange("p a b -> p (a b)"), start=True, stop=True).then_inc(filled, 1)
                out_proj(i, ns + 17, h0 + 8)

            def weigh_values(o, v, n, att):
                nc.tensor.matmul(o[:, 0:T], v[:, 0, n * P:(n + 1) * P], att[:, 0:T], start=True, stop=False, skip_group_check=True)
                return nc.tensor.matmul(o[:, P:T], v[:, 1, n * P:(n + 1) * P], att[:, T:T + P], start=False, stop=True, skip_group_check=True)

            def sb(i, name, prm):
                ns, h0, e = starts[i]["ns"], before(i, "h"), HEADS * before(i, "sb")
                put = lambda label: bank(use[name, label])
                mm = nc.tensor.matmul
                norm_sum(i, name)
                for p in range(8):
                    across(ns + p, put(f"qk{p}"), h_at=h0 if p == 0 else None)
                for p in range(4):
                    along(ns + 8 + p, put(f"v{p}"))
                pe.wait_ge(taken, use[name, "v3"] + 1)
                for n in range(HEADS + 2):
                    if n < HEADS:
                        o = put(f"z{n}")
                        mm(o[:, 0:T], s_k[:, n, 0:P], s_q[:, n, :], start=True, stop=True)
                        mm(o[:, T:T + P], s_k[:, n, P:T], s_q[:, n, P:T], start=True, stop=True).then_inc(filled, 1)
                    if 1 <= n <= HEADS:
                        o, sp = put(f"s{n - 1}"), s_sp[:, (n - 1) % 2, :]
                        pe.wait_ge(taken, use[name, f"z{n - 1}"] + 1)
                        mm(o[:, T:T + P], cst("suffix"), sp[:, T:T + P], start=True, stop=True)
                        mm(o[:, 0:T], cst("suffix"), sp[:, 0:T], start=True, stop=False, skip_group_check=True)
                        mm(o[:, P:T], cst("ones"), sp[:, T:T + P], start=False, stop=True, skip_group_check=True).then_inc(filled, 1)
                    if n >= 2:
                        pe.wait_ge(stage("sb_att"), e + n - 1)
                        weigh_values(put(f"o{n - 2}"), s_v, n - 2, s_att[:, (n - 2) % 3, :]).then_inc(filled, 1)
                out_proj(i, ns + 12, h0 + 8)

            def dsa(i, name, prm):
                ns, h0 = starts[i]["ns"], before(i, "h")
                put = lambda label: bank(use[name, label])
                held = lambda label: pe.wait_ge(taken, use[name, label] + 1)
                mm, tr = nc.tensor.matmul, nc.tensor.transpose
                norm_sum(i, name)
                for p in range(4):
                    across(ns + p, put(f"p{p}"), h_at=h0 if p == 0 else None)
                pe.wait_ge(stage("dsa_sq"), 1)
                o = put("n1")
                for k in range(3):
                    mm(o[:, 0:T], cst("ones"), h[:, k, :], start=(k == 0), stop=(k == 2))
                for k in range(3, 5):
                    m = mm(o[:, T:NB], cst("ones"), h[:, k, :], start=(k == 3), stop=(k == 4))
                m.then_inc(filled, 1)
                mm(put("n2")[:, 0:T], cst("half_ones"), h[:, 6, :], start=True, stop=True).then_inc(filled, 1)
                pe.wait_ge(stage("dsa_ki"), 1)
                o = put("kr")
                mm(o[:, 0:T], cst("rope_q"), d_c[:, 5, :], start=True, stop=True)
                mm(o[:, T:NB], cst("rope_i"), d_c[:, 6, :], start=True, stop=True).then_inc(filled, 1)
                o = put("wt")
                for t in range(2):
                    m = tr(o[:, t * P:(t + 1) * P], d_c[:, 7, t * P:(t + 1) * P], cst("ident"))
                m.then_inc(filled, 1)

                def grouped(ns, kc, k0, width, labels, h_at=None, along_=False):
                    pe.wait_ge(lo_ready, ns + 1)
                    s = ns % SLOTS
                    for gi, label in enumerate(labels):
                        o = put(label)
                        for q in range(kc):
                            if h_at is not None:
                                pe.wait_ge(h_lo_ready, h_at + q + 1)
                            for b in range(2):
                                if along_:
                                    m = products(o[:, b * 256:(b + 1) * 256],
                                                 (h_hi[:, k0 + q, b * P:(b + 1) * P], h_lo[:, k0 + q, b * P:(b + 1) * P]),
                                                 slab(s, q * width + gi * 256, 256), q == 0 and b == 0, q == kc - 1)
                                else:
                                    m = products(o[:, b * T:(b + 1) * T], slab(s, q * width + gi * 256 + b * P),
                                                 (h_hi[:, k0 + q, :], h_lo[:, k0 + q, :]), q == 0 and b == 0, q == kc - 1)
                        m.then_inc(w_used if gi == len(labels) - 1 else filled, 1)

                grouped(ns + 4, 3, 0, 512, ["qi0", "qi1"], h_at=h0 + 8)
                for p in range(2):
                    held(f"qi{p}")
                    mm(put(f"ri{p}"), cst("rope_i"), d_qi[:, 2 * p:2 * p + 2, :], start=True, stop=True).then_inc(filled, 1)
                grouped(ns + 5, 3, 0, 512, ["q0", "q1"])
                grouped(ns + 6, 3, 0, 512, ["q2", "q3"])
                pe.wait_ge(stage("dsa_rot"), 3)
                for n in range(HEADS):
                    o, r = put(f"lg{n}"), slice(64 * (n % 2), 64 * (n % 2) + 64)
                    q, k = d_qi[r, n // 2, :], d_c[r, 6, :]
                    mm(o[:, 0:P], q[:, 0:P], k[:, 0:P], start=True, stop=True)
                    mm(o[:, P:BLK], q[:, P:T], k, start=True, stop=True).then_inc(filled, 1)
                pe.wait_ge(h_lo_ready, h0 + 13)
                grouped(ns + 7, 2, 3, D, [f"k{p}" for p in range(4)])
                grouped(ns + 8, 2, 3, D, [f"v{p}" for p in range(4)], along_=True)
                for p in range(4):
                    mm(put(f"rq{p}"), cst("rope_q"), d_q[:, 2 * p:2 * p + 2, :], start=True, stop=True).then_inc(filled, 1)
                pe.wait_ge(stage("dsa_rot"), 7)
                for n in range(HEADS + 2):
                    if n < HEADS:
                        o = put(f"a{n}")
                        mm(o[:, 0:P], d_q[:, n, 0:P], d_k[:, n, 0:P], start=True, stop=True)
                        mm(o[:, P:BLK], d_q[:, n, P:T], d_k[:, n, :], start=True, stop=True).then_inc(filled, 1)
                    if 1 <= n <= HEADS:
                        pe.wait_ge(stage("dsa_p"), n)
                        o = put(f"t{n - 1}")
                        for b in range(3):
                            m = tr(o[:, b * P:(b + 1) * P], d_p[:, (n - 1) % 3, b * P:(b + 1) * P], cst("ident"))
                        m.then_inc(filled, 1)
                    if n >= 2:
                        held(f"t{n - 2}")
                        weigh_values(put(f"o{n - 2}"), d_v, n - 2, d_pt[:, (n - 2) % 2, :]).then_inc(filled, 1)
                out_proj(i, ns + 9, h0 + 13)

            def attn(i, name, prm):
                ns, h0 = starts[i]["ns"], before(i, "h")
                put = lambda label: bank(use[name, label])
                held = lambda label: pe.wait_ge(taken, use[name, label] + 1)
                mm, tr = nc.tensor.matmul, nc.tensor.transpose

                def project(q, label, h_at=None):
                    if label[0] == "v":
                        along(ns + q, put(label))
                    else:
                        across(ns + q, put(label), h_at=h_at)

                norm_sum(i, name, "norm_c")
                for q, label in enumerate(CTX_PROJ):
                    if q == 4:
                        norm_sum(i, name, "norm", 1)
                    project(q, label, h0 if q == 0 else None)
                for q, label in enumerate(LAT_PROJ):
                    project(8 + q, label, h0 + 8 if q == 0 else None)
                    if label == "kb1":
                        held("qb1")
                        for p in range(2):
                            mm(put(f"rq{p}"), cst("rope_d"), f_q[:, 2 * p:2 * p + 2, :], start=True, stop=True).then_inc(filled, 1)
                for p in range(2):
                    mm(put(f"rk{p}"), cst("rope_d"), f_k[:, 2 * p:2 * p + 2, 0:T], start=True, stop=True).then_inc(filled, 1)
                pe.wait_ge(stage("at_rot"), 4)
                held("rk1")
                for n in range(len(UNITS) + 2):
                    if n < NDIFF:
                        _, hd, t = UNITS[n]
                        for m, label in enumerate((f"s{n}", f"r{n}")):
                            r = slice(64 * m, 64 * m + 64)
                            mm(put(label), f_q[r, hd, t * P:(t + 1) * P], f_k[r, hd, :], start=True, stop=True).then_inc(filled, 1)
                    elif n < len(UNITS):
                        _, hd, t = UNITS[n]
                        r, o = slice(64 * (hd % 2), 64 * (hd % 2) + 64), put(f"s{n}")
                        mm(o, n_q[r, hd // 2, t * P:(t + 1) * P], n_k[r, hd // 2, :], start=True, stop=False, skip_group_check=True)
                        pe.wait_ge(stage("at_bias"), hd + 1)
                        b = n_bias[:, 2 * (hd % 4) + t, :]
                        mm(o[:, 0:T], cst("ident"), b, start=False, stop=True, skip_group_check=True).then_inc(filled, 1)
                    if 1 <= n <= len(UNITS):
                        pe.wait_ge(stage("at_p"), n)
                        o = put(f"t{n - 1}")
                        for b in range(4):
                            m = tr(o[:, b * P:(b + 1) * P], a_p[:, (n - 1) % 3, b * P:(b + 1) * P], cst("ident"))
                        m.then_inc(filled, 1)
                    if n >= 2:
                        held(f"t{n - 2}")
                        kind, hd, t = UNITS[n - 2]
                        o = put(f"o{n - 2}")
                        if kind == "near":
                            o, v, w = o[64 * (hd % 2):64 * (hd % 2) + 64, :], n_v, slice(64 * hd, 64 * hd + 64)
                        else:
                            v, w = f_v, slice(P * hd, P * hd + P)
                        for b in range(4):
                            m = mm(o[:, 0:P], v[:, b, w], a_pt[:, (n - 2) % 2, b * P:(b + 1) * P], start=(b == 0), stop=(b == 3))
                        m.then_inc(filled, 1)
                    if n == SUBLN:
                        pe.wait_ge(stage("at_sq"), 1)
                        for g in range(2):
                            mm(put(f"dn{g}"), cst("ones"), f_sq[:, g * NB:(g + 1) * NB], start=True, stop=True).then_inc(filled, 1)
                out_proj(i, ns + 20, h0 + 16)

            def conv(i, name, prm):
                ns, h0 = starts[i]["ns"], before(i, "h")
                norm_sum(i, name)
                for p in range(4):
                    for k, n in enumerate(("cg", "hh", "bg")):
                        across(ns + 3 * p + k, bank(use[name, f"{n}{p}"]), h_at=h0 if p == k == 0 else None)
                out_proj(i, ns + 12, h0 + 8)

            pe.wait_ge(loaded, 16 * LOADS)
            for i, (kind, name, prm) in enumerate(ops):
                dict(ffn=ffn, mod=mod, final=final, gdn=gdn, sb=sb, dsa=dsa, attn=attn, conv=conv
                     )[kind](i, name, prm)

        @block.scalar
        def _(act):
            static = lambda a, k: a
            steps = Chain(act, act_steps)
            nc.scalar.preload_act_table_set("natural_log_exp_and_others")

            def fn(o, i, f, **kw):
                return nc.scalar.activation(o, i, f, **kw)

            def hi(ns, at=static, k=0):
                n = first_split[ns]
                act.wait_ge(landed[n % SLOTS], at(16 * (n // SLOTS + 1), 16 * k // SLOTS))
                if ns >= SLOTS:
                    act.wait_ge(w_used, at(ns - SLOTS + 1, k))
                fn(w_hi[:, ns % SLOTS, :], raw[:, n % SLOTS, :], ACT.Copy).then_inc(hi_ready, 1)

            done = [0]

            def split_to(ns):
                while done[0] <= min(ns, total["ns"] - 1):
                    hi(done[0])
                    done[0] += 1

            def frees(u):
                if u:
                    act.wait_ge(taken, u)

            def squares(i, nth=0, src=None):
                xs, ready, count = src or stream(i)
                q0 = before(i, "h")
                if q0 + nth:
                    act.wait_ge(h_lo_ready, q0 + KC * nth)
                if xs is c and not count:
                    act.wait_ge(c_loaded, 16)
                for m in range(KC // 2):
                    if count:
                        act.wait_ge(ready, count - KC + 2 * (m + 1))
                    fn(sq[:, 2 * m:2 * m + 2, :], xs[:, 2 * m:2 * m + 2, :], ACT.Square).then_inc(sq_ready, 1)

            def inverse_root(name, label):
                u = use[name, label]
                wait_full(act, name, label)
                frees(u)
                fn(rstd[:, 0:T], wrk[:, u % BANKS, 0:T], ACT.Ln, scale=1.0 / D, bias=EPS).then_inc(taken, 1)
                act.wait_ge(taken, u + 1)
                fn(rstd[:, 0:T], rstd[:, 0:T], ACT.Exp, scale=-0.5).then_inc(rstd_ready, 1)

            def h_high(h0, ks=range(KC)):
                for k in ks:
                    act.wait_ge(h_ready, h_writes(h0) + k + 1)
                    fn(h_hi[:, k, :], h[:, k, :], ACT.Copy).then_inc(h_hi_ready, 1)

            def ffn(i, name, prm):
                ns, u0 = starts[i]["ns"], starts[i]["u"] + 1
                hid0 = STEPS * before(i, "ffn")
                split_to(ns)
                squares(i)
                split_to(ns + 1)
                inverse_root(name, "norm")
                h_high(before(i, "h"))
                split_to(ns + 2)

                def exp_gate(st, at):
                    act.wait_ge(w_used, at(ns + (2 + 3 * (st - 1) if st else 0) + 1, 6))
                    fn(e_gate[:, (hid0 + st) % 2, :], wrk[:, (u0 + 2 * st) % BANKS, :], ACT.Exp, scale=-1.0).then_inc(e_ready, 1)

                def hid_high(st, at):
                    act.wait_ge(taken, at(u0 + 2 * st + 2, 4))
                    if st >= 2:
                        act.wait_ge(w_used, at(ns + 3 * st - 1, 6))
                    q = (hid0 + st) % 2
                    fn(hid_hi[:, q, :], hid[:, q, :], ACT.Copy).then_inc(hid_hi_ready, 1)

                def step(st, at):
                    q = ns + 2 + 3 * (st - 1)
                    hi(q + 1, at, 6)
                    exp_gate(st - 1, at)
                    hid_high(st - 1, at)
                    hi(q + 2, at, 6)
                    hi(q + 3, at, 6)

                step(1, static)
                step(2, static)
                with act.Fori(0, (STEPS - 3) // 2) as r:
                    for st in (3, 4):
                        step(st, lambda a, k: r * k + a)
                done[0] = ns + 3 * STEPS
                exp_gate(STEPS - 1, static)
                hid_high(STEPS - 1, static)

            def mod(i, name, prm):
                if before(i, "mod") == 0:
                    fn(small[:, 0:2 * KC], col("c", 0, 2 * KC), ACT.Exp, scale=-1.0).then_inc(silu_e, 1)

            def final(i, name, prm):
                squares(i)
                inverse_root(name, "norm")


            def gdn(i, name, prm):
                ns, g, j = starts[i]["ns"], before(i, "gdn_ops"), prm["j"]
                bk = lambda label: wrk[:, use[name, label] % BANKS, :]
                full = lambda label: wait_full(act, name, label)
                done_ = lambda label: act.wait_ge(taken, use[name, label] + 1)
                split_to(ns)
                squares(i)
                split_to(ns + 1)
                inverse_root(name, "norm")
                h_high(before(i, "h"))
                split_to(ns + 2)
                full("gates")
                frees(use[name, "gates"])
                b = bk("gates")
                steps.mark(fn(rstd[32:40, 0:T], b[32:40, 0:T], ACT.Exp, scale=-1.0))
                fn(rstd[0:8, T:NB], b[0:8, 0:T], ACT.Identity, bias=col(f"gdn_dt_bias{j}")[0:8]).then_inc(taken, 1)
                done_("gates")
                steps.link(fn(rstd[0:8, 0:T], rstd[0:8, T:NB], ACT.Abs))
                steps.link(fn(rstd[0:8, 0:T], rstd[0:8, 0:T], ACT.Exp, scale=-1.0))
                steps.mark(fn(rstd[0:8, 0:T], rstd[0:8, 0:T], ACT.Ln, bias=1.0))
                fn(small[0:8, 40:41], col(f"gdn_a_log{j}")[0:8], ACT.Exp).then_inc(stage("gdn_gate_parts"), 1)
                steps.wait()
                nc.scalar.preload_act_table_set("silu_and_others")
                wq = lambda p, b, tap: col(f"gdn_conv{j}", tap * 24 + 2 * p + b)
                dst = (g_q, g_k, g_v)

                def silu(p):
                    done_(f"qkv{p}")
                    v = dst[p // 4][:, 2 * (p % 4):2 * (p % 4) + 2, :]
                    fn(v, v, ACT.Silu).then_inc(stage("gdn_silu"), 1)

                for p in range(12):
                    split_to(ns + 3 + p)
                    full(f"qkv{p}")
                    for b in range(2):
                        m = fn(dst[p // 4][:, 2 * (p % 4) + b, :], bk(f"qkv{p}")[:, b * T:(b + 1) * T], ACT.Copy, scale=wq(p, b, 3))
                        if b == 0:
                            steps.mark(m)
                    m.then_inc(stage("gdn_tap"), 1)
                    if p:
                        silu(p - 1)
                silu(11)
                for p in range(4):
                    split_to(ns + 15 + p)
                    full(f"z{p}")
                    frees(use[name, f"z{p}"])
                    fn(g_z[:, 2 * p:2 * p + 2, :].rearrange("p a b -> p (a b)"), bk(f"z{p}"), ACT.Silu).then_inc(taken, 1)
                nc.scalar.preload_act_table_set("natural_log_exp_and_others")
                act.wait_ge(stage("gdn_silu"), 12 * (g + 1))

                def sq_qk(n):
                    if n >= 2:
                        full(f"ss{n - 2}")
                    if n in (0, HALF):
                        act.wait_ge(h_lo_ready, before(i, "h") + (8 if n == 0 else 8 + HALF))
                    steps.mark(fn(h[:, 2 * (n % 2), :], g_q[:, n, :], ACT.Square))
                    fn(h[:, 2 * (n % 2) + 1, :], g_k[:, n, :], ACT.Square).then_inc(stage("gdn_sq"), 1)

                def norm_qk(n):
                    full(f"ss{n}")
                    frees(use[name, f"ss{n}"])
                    if n:
                        act.wait_ge(stage("gdn_qk"), 2 * (8 * g + n))
                    fn(rstd[:], bk(f"ss{n}"), ACT.Ln, bias=EPS).then_inc(taken, 1)
                    done_(f"ss{n}")
                    fn(rstd[:], rstd[:], ACT.Exp, scale=-0.5).then_inc(stage("gdn_rr"), 1)

                for half in range(2):
                    k = 2 * g + half
                    heads = range(half * HALF, half * HALF + HALF)
                    sq_qk(heads[0])
                    for n in heads:
                        if n == heads[0]:
                            norm_qk(n)
                        if n < heads[-1]:
                            sq_qk(n + 1)
                        full(f"rows{n}")
                        if n >= 2:
                            act.wait_ge(stage("gdn_lt"), 8 * g + n - 1)
                        fn(g_eg[:, n % 2, :], bk(f"rows{n}")[:, P:T], ACT.Exp).then_inc(stage("gdn_eg"), 1)
                        done_(f"rows{n}")
                        fn(h[:, 6 + n % 2, :], h[:, 6 + n % 2, :], ACT.Exp).then_inc(stage("gdn_ed"), 1)
                        if n < heads[-1]:
                            norm_qk(n + 1)
                    def copy_out(label, to):
                        full(label)
                        frees(use[name, label])
                        fn(to.rearrange("p a b -> p (a b)"), bk(label), ACT.Copy).then_inc(taken, 1)

                    for a, grp in enumerate("AB"):
                        copy_out(f"vt{half}{grp}", g_vi[:, 4 * a:4 * a + 4, :])
                    for lv in range(len(LEVELS)):
                        for a, grp in enumerate("AB"):
                            copy_out(f"X{half}{lv}{grp}", g_xs[:, 4 * a:4 * a + 4, :])
                    copy_out(f"u0_{half}", g_u0)
                    copy_out(f"S_{half}", g_s)
                    copy_out(f"u1_{half}", g_vi[:, 0:4, :])
                    for q in range(2):
                        done_(f"o{half}{q}")
                        n = half * HALF + 2 * q
                        fn(g_lts[:, q, 0:4, :].rearrange("p a b -> p (a b)"), g_v[:, n:n + 2, :].rearrange("p a b -> p (a b)"),
                           ACT.Square).then_inc(stage("gdn_osq"), 1)
                    for q in range(2):
                        label = f"os{half}{q}"
                        full(label)
                        frees(use[name, label])
                        act.wait_ge(stage("gdn_on"), 2 * k + q)
                        fn(rstd[:], bk(label), ACT.Ln, scale=1.0 / HD, bias=EPS).then_inc(taken, 1)
                        done_(label)
                        fn(rstd[:], rstd[:], ACT.Exp, scale=-0.5).then_inc(stage("gdn_orr"), 1)
                        h_high(before(i, "h") + 8, range(half * HALF + 2 * q, half * HALF + 2 * q + 2))
                split_to(ns + 20)

            def opening(i, name):
                ns = starts[i]["ns"]
                split_to(ns)
                squares(i)
                split_to(ns + 1)
                inverse_root(name, "norm")
                h_high(before(i, "h"))
                split_to(ns + 2)

            def sb(i, name, prm):
                ns, h0 = starts[i]["ns"], before(i, "h")
                opening(i, name)
                for p in range(12):
                    split_to(ns + 3 + p)
                for n in range(HEADS + 2):
                    if n < HEADS:
                        wait_full(act, name, f"z{n}")
                        if n >= 2:
                            act.wait_ge(taken, use[name, f"z{n - 2}"] + 1)
                        l = s_l[:, n % 2, :]
                        steps.link(fn(l, wrk[:, use[name, f"z{n}"] % BANKS, 0:T + P], ACT.Abs))
                        steps.link(fn(l, l, ACT.Exp, scale=-1.0))
                        fn(l, l, ACT.Ln, bias=1.0).then_inc(stage("sb_l"), 1)
                    if 1 <= n <= HEADS:
                        act.wait_ge(taken, use[name, f"s{n - 1}"] + 1)
                        a = s_att[:, (n - 1) % 3, :]
                        fn(a, a, ACT.Exp).then_inc(stage("sb_exp"), 1)
                    if n >= 2:
                        act.wait_ge(taken, use[name, f"o{n - 2}"] + 1)
                        fn(h_hi[:, n - 2, :], h[:, n - 2, :], ACT.Copy).then_inc(h_hi_ready, 1)
                split_to(ns + 15)

            def dsa(i, name, prm):
                ns, h0 = starts[i]["ns"], before(i, "h")
                bk = lambda label: wrk[:, use[name, label] % BANKS, :]
                full = lambda label: wait_full(act, name, label)
                held = lambda label: act.wait_ge(taken, use[name, label] + 1)
                opening(i, name)
                split_to(ns + 5)
                held("p3")
                fn(h[:, 0:7, :], d_c[:, 0:7, :], ACT.Square).then_inc(stage("dsa_sq"), 1)
                full("n1")
                frees(use[name, "n1"])
                steps.mark(fn(rstd[:, 0:T], bk("n1")[:, 0:T], ACT.Ln, scale=1.0 / 384, bias=EPS))
                fn(rstd[:, T:NB], bk("n1")[:, T:NB], ACT.Ln, scale=1.0 / 256, bias=EPS).then_inc(taken, 1)
                held("n1")
                fn(rstd[:], rstd[:], ACT.Exp, scale=-0.5).then_inc(stage("dsa_rr"), 1)
                full("n2")
                frees(use[name, "n2"])
                fn(d_r, bk("n2")[:, 0:T], ACT.Ln, scale=1.0 / 64, bias=EPS).then_inc(taken, 1)
                held("n2")
                fn(d_r, d_r, ACT.Exp, scale=-0.5).then_inc(stage("dsa_rr"), 1)
                h_high(h0 + 8, range(5))
                split_to(ns + 6)
                split_to(ns + 7)
                for n in range(HEADS):
                    full(f"lg{n}")
                    frees(use[name, f"lg{n}"])
                    if n >= 2:
                        act.wait_ge(stage("dsa_score"), n - 1)
                    fn(d_t[:, n % 2, :], bk(f"lg{n}")[:, 0:BLK], ACT.Relu).then_inc(taken, 1)
                split_to(ns + 9)
                split_to(ns + 11)
                for n in range(HEADS + 2):
                    if n < HEADS:
                        act.wait_ge(stage("dsa_max"), n + 1)
                        st = 32 + 8 * (n % 2)
                        for t, (a, b) in enumerate(((0, P), (P, BLK))):
                            v = d_p[:, n % 3, a:b]
                            m = fn(v, v, ACT.Exp, bias=small[:, st + t:st + t + 1], accum_out=small[:, st + 2 + t:st + 3 + t])
                            if t == 0:
                                steps.mark(m)
                        m.then_inc(stage("dsa_exp"), 1)
                    if 1 <= n <= HEADS:
                        full(f"t{n - 1}")
                        frees(use[name, f"t{n - 1}"])
                        if n >= 3:
                            full(f"o{n - 3}")
                        fn(d_pt[:, (n - 1) % 2, :], bk(f"t{n - 1}")[:, 0:BLK], ACT.Copy).then_inc(taken, 1)
                    if n >= 2:
                        held(f"o{n - 2}")
                        fn(h_hi[:, n - 2, :], h[:, n - 2, :], ACT.Copy).then_inc(h_hi_ready, 1)
                split_to(ns + 12)

            def attn(i, name, prm):
                ns, h0 = starts[i]["ns"], before(i, "h")
                bk = lambda label: wrk[:, use[name, label] % BANKS, :]
                full = lambda label: wait_full(act, name, label)
                split_to(ns)
                squares(i, src=(c, c_new, before(i, "c")))
                split_to(ns + 1)
                inverse_root(name, "norm_c")
                h_high(h0)
                split_to(ns + 4)
                squares(i, nth=1)
                split_to(ns + 5)
                inverse_root(name, "norm")
                split_to(ns + 10)
                act.wait_ge(w_used, ns + 8)
                h_high(h0 + 8)
                act.wait_ge(stage("at_lam"), 1)
                fn(small[:, 62:64], small[:, 60:62], ACT.Exp).then_inc(stage("at_lam_e"), 1)
                split_to(ns + 22)
                for n in range(len(UNITS) + 2):
                    st = 32 + 8 * (n % 2)
                    if n < len(UNITS):
                        act.wait_ge(stage("at_max"), n + 1)
                        if n >= 2:
                            act.wait_ge(stage("at_p"), n - 1)
                        frees(use[name, f"s{n}"])
                        fn(a_p[:, n % 3, :], bk(f"s{n}"), ACT.Exp, bias=small[:, st:st + 1],
                           accum_out=small[:, st + 2:st + 3]).then_inc(taken, 1)
                        if n < NDIFF:
                            fn(a_p1[:, n % 2, :], bk(f"r{n}"), ACT.Exp, bias=small[:, st + 1:st + 2],
                               accum_out=small[:, st + 3:st + 4]).then_inc(taken, 1)
                    if 1 <= n <= len(UNITS):
                        full(f"t{n - 1}")
                        frees(use[name, f"t{n - 1}"])
                        if n >= 3:
                            full(f"o{n - 3}")
                        fn(a_pt[:, (n - 1) % 2, :], bk(f"t{n - 1}"), ACT.Copy).then_inc(taken, 1)
                    if n == SUBLN - 1:
                        act.wait_ge(taken, use[name, f"o{NDIFF - 1}"] + 1)
                        fn(f_sq, h[:, 0:4, :].rearrange("p a b -> p (a b)"), ACT.Square).then_inc(stage("at_sq"), 1)
                    if n == SUBLN:
                        for g in range(2):
                            full(f"dn{g}")
                            frees(use[name, f"dn{g}"])
                            fn(f_rr[:, g * NB:(g + 1) * NB], bk(f"dn{g}"), ACT.Ln, scale=1.0 / P, bias=EPS).then_inc(taken, 1)
                        act.wait_ge(taken, use[name, "dn1"] + 1)
                        fn(f_rr, f_rr, ACT.Exp, scale=-0.5).then_inc(stage("at_rr"), 1)
                    if n == SUBLN + 1:
                        act.wait_ge(stage("at_d"), 1)
                        fn(h_hi[:, 0:4, :], h[:, 0:4, :], ACT.Copy).then_inc(h_hi_ready, 4)
                    if n >= NDIFF + 2 and (n - 2 - NDIFF) % 4 == 3:
                        k = 4 + (n - 2 - NDIFF) // 4
                        act.wait_ge(taken, use[name, f"o{n - 2}"] + 1)
                        fn(h_hi[:, k, :], h[:, k, :], ACT.Copy).then_inc(h_hi_ready, 1)
                split_to(ns + 23)

            def conv(i, name, prm):
                ns, h0 = starts[i]["ns"], before(i, "h")
                opening(i, name)
                for p in range(4):
                    for k, (n, place) in enumerate((("cg", v_cg), ("bg", v_bg))):
                        split_to(ns + 3 * p + 2 * k + 2)
                        wait_full(act, name, f"{n}{p}")
                        frees(use[name, f"{n}{p}"])
                        if p >= 2 and k:
                            act.wait_ge(h_ready, h_writes(h0) + 8 + 2 * (p - 1))
                        fn(place[:, p % 2, :, :].rearrange("p a b -> p (a b)"), wrk[:, use[name, f"{n}{p}"] % BANKS, :],
                           ACT.Copy).then_inc(taken, 1)
                split_to(ns + 14)
                act.wait_ge(w_used, ns + 12)
                h_high(h0 + 8)
                split_to(ns + 15)

            act.wait_ge(loaded, 16 * LOADS)
            for i, (kind, name, prm) in enumerate(ops):
                dict(ffn=ffn, mod=mod, final=final, gdn=gdn, sb=sb, dsa=dsa, attn=attn, conv=conv
                     )[kind](i, name, prm)

        @block.vector
        def _(dve):
            static = lambda a, k: a
            steps = Chain(dve, dve_steps)
            tt, ts, stt = nc.vector.tensor_tensor, nc.vector.tensor_scalar, nc.vector.scalar_tensor_tensor

            def lo(ns, at=static, k=0):
                n = first_split[ns]
                dve.wait_ge(hi_ready, at(ns + 1, k))
                tt(w_lo[:, ns % SLOTS, :], raw[:, n % SLOTS, :], w_hi[:, ns % SLOTS, :].bitcast(F32),
                   ALU.subtract).then_inc(lo_ready, 1)

            done = [0]

            def split_to(ns):
                while done[0] <= min(ns, total["ns"] - 1):
                    lo(done[0])
                    done[0] += 1

            def h_low(h0, k):
                dve.wait_ge(h_hi_ready, h0 + k + 1)
                tt(h_lo[:, k, :], h[:, k, :], h_hi[:, k, :].bitcast(F32), ALU.subtract).then_inc(h_lo_ready, 1)

            def normed(i, prm, nth=0, src=None, low=True):
                xs = (src or stream(i))[0]
                h0 = before(i, "h") + 8 * nth
                if xs is c:
                    dve.wait_ge(c_loaded, 16)
                dve.wait_ge(rstd_ready, before(i, "norm") + nth + 1)
                for k in range(KC + 2):
                    if k < KC:
                        a, b = scale_cols(prm, k)
                        m = stt(h[:, k, :], xs[:, k, :], a, rstd[:, 0:T], ALU.mult, ALU.mult)
                        if b is None:
                            m.then_inc(h_ready, 1)
                        else:
                            steps.mark(m)
                    if b is not None and 1 <= k <= KC:
                        dve.wait_ge(dve_steps, steps.n - (1 if k < KC else 0))
                        ts(h[:, k - 1, :], h[:, k - 1, :], scale_cols(prm, k - 1)[1], None, ALU.add).then_inc(h_ready, 1)
                    if k >= 2 and low:
                        h_low(h0, k - 2)

            def ffn(i, name, prm):
                ns, u0 = starts[i]["ns"], starts[i]["u"] + 1
                hid0 = STEPS * before(i, "ffn")
                split_to(ns + 1)
                normed(i, prm)
                split_to(ns + 2)

                def gated(st, at):
                    q, ug = (hid0 + st) % 2, u0 + 2 * st
                    dve.wait_ge(e_ready, at(hid0 + st + 1, 2))
                    steps.link(ts(hid_t[:, q, :], e_gate[:, q, :], 1.0, None, ALU.add))
                    steps.link(nc.vector.reciprocal(hid_t[:, q, :], hid_t[:, q, :]))
                    tt(hid_t[:, q, :], wrk[:, ug % BANKS, :], hid_t[:, q, :], ALU.mult).then_inc(taken, 1)
                    dve.wait_ge(taken, at(ug + 1, 4))
                    dve.wait_ge(w_used, at(ns + (3 + 3 * (st - 1) if st else 1) + 1, 6))
                    tt(hid[:, q, :], hid_t[:, q, :], wrk[:, (ug + 1) % BANKS, :], ALU.mult).then_inc(taken, 1)

                def hid_low(st, at):
                    q = (hid0 + st) % 2
                    dve.wait_ge(hid_hi_ready, at(hid0 + st + 1, 2))
                    tt(hid_lo[:, q, :], hid[:, q, :], hid_hi[:, q, :].bitcast(F32), ALU.subtract).then_inc(hid_lo_ready, 1)

                def step(st, at):
                    q = ns + 2 + 3 * (st - 1)
                    lo(q + 1, at, 6)
                    gated(st - 1, at)
                    hid_low(st - 1, at)
                    lo(q + 2, at, 6)
                    lo(q + 3, at, 6)

                step(1, static)
                step(2, static)
                n_in = steps.n
                with dve.Fori(0, (STEPS - 3) // 2) as r:
                    steps.at = lambda a: r * 4 + a
                    for st in (3, 4):
                        step(st, lambda a, k: r * k + a)
                assert steps.n == n_in + 4
                steps.at = lambda a: a
                steps.n += 4 * ((STEPS - 3) // 2 - 1)
                done[0] = ns + 3 * STEPS
                gated(STEPS - 1, static)
                hid_low(STEPS - 1, static)
                if done[0] < total["ns"] and kinds[first_split[done[0]] - 1] == "split":
                    split_to(done[0])
                xs, seen = stream(i)[:2]
                for m in range(KC // 2):
                    if m < KC // 2 - 1:
                        dve.wait_ge(acc_full, 3 * before(i, "ffn") + m + 1)
                    else:
                        dve.wait_ge(w_used, ns + 3 * STEPS)
                    if "a" in prm:
                        v = xs[:, 2 * m:2 * m + 2, :].rearrange("p a b -> p (a b)")
                        stt(v, acc[:, m, :], 0.5, v, ALU.mult, ALU.add).then_inc(seen, 2)
                    else:
                        w, j = (0 if prm["x"] == "x" else 1), (3 * prm["s"] + 2) * KC + 2 * m
                        for b in range(2):
                            v = xs[:, 2 * m + b, :]
                            stt(v, acc[:, m, b * T:(b + 1) * T], der[:, prm["l"], w, j + b:j + b + 1], v,
                                ALU.mult, ALU.add).then_inc(seen, 1)

            def mod(i, name, prm):
                l = prm["l"]
                if before(i, "mod") == 0:
                    dve.wait_ge(silu_e, 1)
                    e, cc = small[:, 0:2 * KC], silu_cc[:].rearrange("p a b -> p (a b)")
                    steps.link(ts(e, e, 1.0, None, ALU.add))
                    steps.link(nc.vector.reciprocal(e, e))
                    tt(cc, e, col("c", 0, 2 * KC), ALU.mult).then_inc(silu_c, 1)
                u = use[name, "mod"]
                wait_full(dve, name, "mod")
                for w in range(2):
                    v = wrk[:, u % BANKS, 0:18 * KC].rearrange("p (j w) -> p j w", w=2)[:, :, w]
                    m = tt(der[:, l, w, :], v, col(f"mod_b{l}", 0, 9 * KC), ALU.add)
                    if w == 0:
                        steps.mark(m)
                m.then_inc(taken, 1)
                dve.wait_ge(taken, u + 1)
                steps.wait()
                for w in range(2):
                    for s in range(3):
                        j = 3 * s * KC
                        v = der[:, l, w, j + KC:j + 2 * KC]
                        steps.mark(stt(v, v, 1.0, col(f"norm_g{l}{s}", 0, KC), ALU.add, ALU.mult))
                        if s != 1:
                            v = der[:, l, w, j + 2 * KC:j + 3 * KC]
                            steps.mark(ts(v, v, 0.5, None, ALU.mult))
                steps.wait()

            def final(i, name, prm):
                xs, seen, count = stream(i)
                dve.wait_ge(rstd_ready, before(i, "norm") + 1)
                for k in range(KC):
                    stt(xs[:, k, :], xs[:, k, :], scale_cols(prm, k)[0], rstd[:, 0:T], ALU.mult, ALU.mult).then_inc(seen, 1)


            def add_out(i, ns, gate=None):
                xs, seen = stream(i)[:2]
                for p in range(4):
                    split_to(ns + min(p + 2, 4))
                    dve.wait_ge(w_used, ns + p + 1)
                    if gate is None:
                        v = xs[:, 2 * p:2 * p + 2, :].rearrange("p a b -> p (a b)")
                        tt(v, acc[:, p, :], v, ALU.add).then_inc(seen, 2)
                    else:
                        for q in range(2):
                            v = xs[:, 2 * p + q, :]
                            stt(v, acc[:, p, q * T:(q + 1) * T], gate(2 * p + q), v, ALU.mult, ALU.add).then_inc(seen, 1)

            def gdn(i, name, prm):
                ns, g, j = starts[i]["ns"], before(i, "gdn_ops"), prm["j"]
                bk = lambda label: wrk[:, use[name, label] % BANKS, :]
                full = lambda label: wait_full(dve, name, label)

                def frees(label):
                    dve.wait_ge(taken, use[name, label])

                split_to(ns + 1)
                normed(i, prm)
                split_to(ns + 2)
                dve.wait_ge(stage("gdn_gate_parts"), g + 1)
                nc.vector.memset(g_rows, 0.0).then_inc(dve_steps, 1)
                steps.n += 1
                steps.link(ts(rstd[32:40, 0:T], rstd[32:40, 0:T], 1.0, None, ALU.add))
                steps.mark(nc.vector.reciprocal(g_rows[32:40, :], rstd[32:40, 0:T]))
                steps.link(stt(rstd[0:8, 0:T], rstd[0:8, T:NB], 0.0, rstd[0:8, 0:T], ALU.max, ALU.add))
                steps.link(ts(rstd[0:8, 0:T], rstd[0:8, 0:T], small[0:8, 40:41], -1.0, ALU.mult, ALU.mult))
                for t in range(2):
                    s = slice(t * P, (t + 1) * P)
                    m = nc.vector.tensor_tensor_scan(g_rows[0:8, s], cst("ones")[0:8, :], rstd[0:8, s], 0.0, ALU.mult, ALU.add)
                    if t == 0:
                        steps.mark(m)
                m.then_inc(stage("gdn_gates"), 1)

                wq = lambda p, b, tap: col(f"gdn_conv{j}", tap * 24 + 2 * p + b)
                dst = (g_q, g_k, g_v)
                for p in range(12):
                    dve.wait_ge(stage("gdn_tap"), 12 * g + p + 1)
                    frees(f"qkv{p}")
                    for tap in (2, 1, 0):
                        s = 3 - tap
                        for b in range(2):
                            v = dst[p // 4][:, 2 * (p % 4) + b, :]
                            m = stt(v[:, s:T], bk(f"qkv{p}")[:, b * T:(b + 1) * T - s], wq(p, b, tap), v[:, s:T], ALU.mult, ALU.add)
                            if (tap, b) != (0, 1):
                                steps.mark(m)
                        if tap:
                            steps.wait()
                    m.then_inc(taken, 1)
                    split_to(ns + 3 + p)
                for p in range(4):
                    split_to(ns + 15 + p)
                full("cols")
                frees("cols")
                picked = lambda r: bk("cols")[:, 0:80].rearrange("p (t c) -> p t c", c=40)[:, :, 32 * r:32 * r + 8]
                octets = lambda a: small[:, a:a + 16].rearrange("p (t c) -> p t c", c=8)
                steps.mark(nc.vector.tensor_copy(octets(0), picked(0)))
                steps.mark(nc.vector.tensor_copy(octets(16), picked(1)))
                ts(octets(32), picked(1), -1.0, None, ALU.mult).then_inc(taken, 1)
                dve.wait_ge(taken, use[name, "cols"] + 1)
                decay_col = lambda n, t: small[:, 8 * t + n:8 * t + n + 1]
                beta_col = lambda n, t: small[:, 16 + 8 * t + n:16 + 8 * t + n + 1]
                minus_beta_col = lambda n, t: small[:, 32 + 8 * t + n:32 + 8 * t + n + 1]
                two = lambda v: v.unsqueeze(1).to_broadcast([P, 2, P])
                pair = lambda v: v.rearrange("p (a b) -> p a b", b=P)

                for half in range(2):
                    k = 2 * g + half
                    heads = range(half * HALF, half * HALF + HALF)
                    for n in heads:
                        b_ = n - heads[0]
                        dve.wait_ge(stage("gdn_rr"), 8 * g + n + 1)
                        stt(g_q[:, n, :], g_q[:, n, :], HD ** -0.5, rstd[:, 0:T], ALU.mult, ALU.mult).then_inc(stage("gdn_qk"), 1)
                        tt(g_k[:, n, :], g_k[:, n, :], rstd[:, T:NB], ALU.mult).then_inc(stage("gdn_qk"), 1)
                        dve.wait_ge(stage("gdn_eg"), 8 * g + n + 1)
                        ed, brs, rows = h[:, 6 + n % 2, :], h[:, 4 + n % 2, :], bk(f"rows{n}")
                        frees(f"rows{n}")
                        steps.mark(tt(pair(brs), pair(rows[:, T:NB]), two(cst("strict")), ALU.mult))
                        for t in range(2):
                            m = ts(ed[:, t * P:(t + 1) * P], rows[:, t * P:(t + 1) * P], decay_col(n, t), 0.0, ALU.subtract, ALU.min)
                            if t == 0:
                                steps.mark(m)
                        m.then_inc(taken, 1)
                        dve.wait_ge(stage("gdn_ed"), 8 * g + n + 1)
                        steps.link(tt(pair(ed), pair(ed), two(cst("causal")), ALU.mult))
                        full(f"kk{n}")
                        lt = g_lt[:, 2 * b_:2 * b_ + 2, :].rearrange("p a b -> p (a b)")
                        steps.mark(tt(lt, bk(f"kk{n}")[:, 0:T], ed, ALU.mult))
                        tt(g_qk[:, b_, :], bk(f"kk{n}")[:, T:NB], ed, ALU.mult).then_inc(taken, 1)
                        steps.wait()
                        tt(lt, lt, brs, ALU.mult).then_inc(stage("gdn_lt"), 1)
                        full(f"tr{n}")
                        frees(f"tr{n}")
                        v = bk(f"tr{n}")
                        for t in range(2):
                            steps.mark(ts(g_bv[:, 2 * b_ + t, :], v[:, t * P:(t + 1) * P], beta_col(n, t), None, ALU.mult))
                        ts(g_kd[:, b_, :], v[:, 2 * P:3 * P], ed[:, P - 1:P], None, ALU.mult).then_inc(taken, 1)
                        for a in (g_q, g_k):
                            steps.mark(tt(a[:, n, P:T], a[:, n, P:T], g_eg[:, n % 2, :], ALU.mult))
                    dve.wait_ge(stage("gdn_lt"), 8 * g + heads[-1] + 1)
                    steps.link(tt(g_u, g_lt, cst("levels", 0, P).unsqueeze(1).to_broadcast([P, 8, P]), ALU.mult))
                    tt(g_u, cst("ident").unsqueeze(1).to_broadcast([P, 8, P]), g_u, ALU.subtract).then_inc(stage("gdn_u1"), 1)
                    for lv in range(len(LEVELS)):
                        for a, grp in enumerate("AB"):
                            for label, t in (("Y", g_vi), ("YT", g_u)):
                                if label == "YT" or lv < len(LEVELS) - 1:
                                    l_ = f"{label}{half}{lv}{grp}"
                                    full(l_)
                                    frees(l_)
                                    v = t[:, 4 * a:4 * a + 4, :].rearrange("p a b -> p (a b)")
                                    tt(v, v, bk(l_), ALU.subtract).then_inc(taken, 1)
                    l_ = f"R_{half}"
                    full(l_)
                    frees(l_)
                    for b_ in range(HALF):
                        v = g_bv[:, 2 * b_ + 1, :]
                        m = stt(v, bk(l_)[:, b_ * P:(b_ + 1) * P], minus_beta_col(heads[b_], 1), v, ALU.mult, ALU.add)
                        if b_ < HALF - 1:
                            steps.mark(m)
                    m.then_inc(taken, 1)
                    for q in range(2):
                        l_ = f"o{half}{q}"
                        full(l_)
                        frees(l_)
                        n = heads[2 * q]
                        nc.vector.tensor_copy(g_v[:, n:n + 2, :].rearrange("p a b -> p (a b)"), bk(l_)).then_inc(taken, 1)
                    for q in range(2):
                        n = heads[2 * q]
                        dve.wait_ge(stage("gdn_orr"), 2 * k + q + 1)
                        v = g_v[:, n:n + 2, :].rearrange("p a b -> p (a b)")
                        tt(v, v, rstd[:], ALU.mult).then_inc(stage("gdn_on"), 1)
                        dve.wait_ge(stage("gdn_on"), 2 * k + q + 1)
                        for b in range(2):
                            stt(h[:, n + b, :], g_v[:, n + b, :], col(f"gdn_norm{j}"), g_z[:, n + b, :], ALU.mult, ALU.mult).then_inc(h_ready, 1)
                        for b in range(2):
                            h_low(before(i, "h") + 8, n + b)
                split_to(ns + 18)
                add_out(i, ns + 17)

            def sb(i, name, prm):
                ns, h0, e = starts[i]["ns"], before(i, "h"), HEADS * before(i, "sb")
                split_to(ns + 1)
                normed(i, prm)
                split_to(ns + 2)
                bk = lambda label: wrk[:, use[name, label] % BANKS, :]
                for p in range(8):
                    wait_full(dve, name, f"qk{p}")
                    dst = (s_q, s_k)[p // 4][:, 2 * (p % 4):2 * (p % 4) + 2, :].rearrange("p a b -> p (a b)")
                    if p == 0:
                        dve.wait_ge(taken, use[name, "norm"] + 1)
                    ts(dst, bk(f"qk{p}"), HD ** -0.5 if p < 4 else 1.0, None, ALU.mult).then_inc(taken, 1)
                    split_to(ns + 3 + p)
                for p in range(4):
                    wait_full(dve, name, f"v{p}")
                    nc.vector.tensor_copy(s_v[:, :, p * 256:(p + 1) * 256], bk(f"v{p}").rearrange("p (a b) -> p a b", b=256)).then_inc(taken, 1)
                    split_to(ns + 11 + p)
                diag = lambda a: a.rearrange("p (a b) -> p a b", b=P)[:, 0:3:2, :]
                strict2 = cst("strict").unsqueeze(1).to_broadcast([P, 2, P])
                for n in range(HEADS + 2):
                    if n < HEADS:
                        z, sp, lb = bk(f"z{n}")[:, 0:T + P], s_sp[:, n % 2, :], s_att[:, n % 3, :]
                        dve.wait_ge(stage("sb_l"), e + n + 1)
                        steps.link(stt(sp, z, 0.0, s_l[:, n % 2, :], ALU.max, ALU.add))
                        tt(lb, z, sp, ALU.subtract).then_inc(dve_steps, 1)
                        steps.n += 1
                        steps.wait()
                        tt(diag(sp), diag(sp), strict2, ALU.mult).then_inc(taken, 1)
                    if 1 <= n <= HEADS:
                        wait_full(dve, name, f"s{n - 1}")
                        a = s_att[:, (n - 1) % 3, :]
                        tt(a, a, bk(f"s{n - 1}")[:, 0:T + P], ALU.subtract).then_inc(taken, 1)
                    if n >= 2:
                        wait_full(dve, name, f"o{n - 2}")
                        nc.vector.tensor_copy(h[:, n - 2, :], bk(f"o{n - 2}")[:, 0:T]).then_inc(taken, 1)
                    if 1 <= n <= HEADS:
                        dve.wait_ge(stage("sb_exp"), e + n)
                        tt(diag(a), diag(a), strict2, ALU.mult).then_inc(stage("sb_att"), 1)
                    if n >= 2:
                        h_low(h0 + 8, n - 2)
                add_out(i, ns + 12)

            def rotate(pairs, swapped, sin, cos, end, place=d_tmp):
                n = len(pairs)
                tmp = place.rearrange("p (a b) -> p a b", b=T)
                for j in range(n):
                    m = tt(tmp[:, j, :], swapped[:, j * T:(j + 1) * T], sin[j], ALU.mult)
                    if j < n - 1:
                        steps.mark(m)
                m.then_inc(taken, 1)
                for j in range(n):
                    steps.mark(tt(pairs[j], pairs[j], cos[j], ALU.mult))
                dve.wait_ge(taken, end)
                steps.wait()
                for j in range(n):
                    m = tt(pairs[j], pairs[j], tmp[:, j, :], ALU.add)
                    if j < n - 1:
                        steps.mark(m)
                return m

            def dsa(i, name, prm):
                ns, h0 = starts[i]["ns"], before(i, "h")
                bk = lambda label: wrk[:, use[name, label] % BANKS, :]
                full = lambda label: wait_full(dve, name, label)
                after = lambda label: dve.wait_ge(taken, use[name, label] + 1)
                two_chunks = lambda a, p: a[:, 2 * p:2 * p + 2, :].rearrange("p a b -> p (a b)")
                split_to(ns + 1)
                normed(i, prm)
                split_to(ns + 2)
                after("norm")
                for p in range(4):
                    full(f"p{p}")
                    nc.vector.tensor_copy(two_chunks(d_c, p), bk(f"p{p}")).then_inc(taken, 1)
                    split_to(ns + min(3 + p, 5))
                dve.wait_ge(stage("dsa_rr"), 2)
                stt(d_c[:, 6, :], d_c[:, 6, :], col("dsa_kidx_norm"), d_r, ALU.mult, ALU.mult).then_inc(stage("dsa_ki"), 1)
                for k in range(5):
                    g_ = col("dsa_cq_norm", k) if k < 3 else col("dsa_ckv_norm", k - 3)
                    stt(h[:, k, :], d_c[:, k, :], g_, rstd[:, (k // 3) * T:(k // 3 + 1) * T], ALU.mult, ALU.mult).then_inc(h_ready, 1)
                for k in range(5):
                    h_low(h0 + 8, k)
                full("kr")
                dve.wait_ge(stage("dsa_ki"), 1)
                rotate([d_c[:, 5, :], d_c[:, 6, :]], bk("kr"), (cst("sin_q"), cst("sin_i")), (cst("cos_q"), cst("cos_i")),
                       use[name, "kr"] + 1).then_inc(stage("dsa_rot"), 1)
                full("wt")
                ts(small[:, 0:16].rearrange("p (a b) -> p a b", b=8), bk("wt")[:, 0:T].rearrange("p (a b) -> p a b", b=P)[:, :, 0:8],
                   HEADS ** -0.5 * 64 ** -0.5, None, ALU.mult).then_inc(taken, 1)
                for p in range(2):
                    full(f"qi{p}")
                    nc.vector.tensor_copy(two_chunks(d_qi, p), bk(f"qi{p}")).then_inc(taken, 1)
                for p in range(2):
                    full(f"ri{p}")
                    if p == 0:
                        after("qi1")
                    rotate([d_qi[:, 2 * p, :], d_qi[:, 2 * p + 1, :]], bk(f"ri{p}"), [cst("sin_i")] * 2, [cst("cos_i")] * 2,
                           use[name, f"ri{p}"] + 1).then_inc(stage("dsa_rot"), 1)
                    dve.wait_ge(stage("dsa_rot"), 2 + p)
                split_to(ns + 6)
                split_to(ns + 7)
                for p in range(4):
                    full(f"q{p}")
                    ts(two_chunks(d_q, p), bk(f"q{p}"), 128 ** -0.5, None, ALU.mult).then_inc(taken, 1)
                for n in range(HEADS):
                    after(f"lg{n}")
                    for t, (a, b) in enumerate(((0, P), (P, BLK))):
                        w_ = small[:, 8 * t + n:8 * t + n + 1]
                        if n == 0:
                            m = ts(d_score[:, a:b], d_t[:, 0, a:b], w_, None, ALU.mult)
                        else:
                            if t == 0:
                                dve.wait_ge(stage("dsa_score"), n)
                            m = stt(d_score[:, a:b], d_t[:, n % 2, a:b], w_, d_score[:, a:b], ALU.mult, ALU.add)
                        if t == 0:
                            steps.mark(m)
                    m.then_inc(stage("dsa_score"), 1)
                split_to(ns + 8)
                for p in range(4):
                    full(f"k{p}")
                    kr = d_c[:, 5, :].unsqueeze(1).to_broadcast([P, 2, T])
                    tt(d_k[:, 2 * p:2 * p + 2, :], bk(f"k{p}").rearrange("p (a b) -> p a b", b=T), kr, ALU.add).then_inc(taken, 1)
                for p in range(4):
                    full(f"v{p}")
                    nc.vector.tensor_copy(d_v[:, :, p * 256:(p + 1) * 256], bk(f"v{p}").rearrange("p (a b) -> p a b", b=256)).then_inc(taken, 1)
                split_to(ns + 9)
                for p in range(4):
                    full(f"rq{p}")
                    rotate([d_q[:, 2 * p, :], d_q[:, 2 * p + 1, :]], bk(f"rq{p}"), [cst("sin_q")] * 2, [cst("cos_q")] * 2,
                           use[name, f"rq{p}"] + 1).then_inc(stage("dsa_rot"), 1)
                    dve.wait_ge(stage("dsa_rot"), 4 + p)
                split_to(ns + 11)
                dve.wait_ge(stage("dsa_score"), HEADS)
                seen = [cst("above", 0, P), cst("above", T, 2 * T)]
                cut = ((0, P), (P, BLK))
                for t, (a, b) in enumerate(cut):
                    steps.mark(ts(d_mask[:, a:b], seen[t], -1.0, 1e38, ALU.add, ALU.mult))
                    steps.mark(tt(d_score[:, a:b], d_score[:, a:b], seen[t], ALU.mult))
                steps.wait()
                steps.link(tt(d_score, d_score, d_mask, ALU.add))
                for _ in range(TOPK // 8):
                    for t, (a, b) in enumerate(cut):
                        steps.mark(nc.vector.max(small[:, 16 + 8 * t:24 + 8 * t], d_score[:, a:b]))
                    steps.wait()
                    for t, (a, b) in enumerate(cut):
                        steps.mark(nc.vector.match_replace(d_score[:, a:b], small[:, 16 + 8 * t:24 + 8 * t], d_score[:, a:b], -3e38))
                    steps.wait()
                steps.link(ts(d_score, d_score, -2e38, None, ALU.is_le))
                for t, (a, b) in enumerate(cut):
                    steps.mark(tt(d_score[:, a:b], d_score[:, a:b], seen[t], ALU.mult))
                steps.wait()
                steps.link(ts(d_mask, d_score, -1.0, 1e30, ALU.add, ALU.mult))

                for n in range(HEADS + 2):
                    if n < HEADS:
                        full(f"a{n}")
                        p_, st = d_p[:, n % 3, :], 32 + 8 * (n % 2)
                        if n >= 3:
                            after(f"t{n - 3}")
                        if n >= 2:
                            dve.wait_ge(taken, use[name, f"a{n}"])
                        tt(p_, bk(f"a{n}")[:, 0:BLK], d_mask, ALU.add).then_inc(taken, 1)
                        after(f"a{n}")
                        for t, (a, b) in enumerate(cut):
                            m = nc.vector.tensor_reduce(small[:, st + t:st + t + 1], p_[:, a:b], AX.X, ALU.max, negate=True)
                            if t == 0:
                                steps.mark(m)
                        m.then_inc(stage("dsa_max"), 1)
                    if n >= 2:
                        full(f"o{n - 2}")
                        dve.wait_ge(taken, use[name, f"o{n - 2}"])
                        nc.vector.tensor_copy(h[:, n - 2, :], bk(f"o{n - 2}")[:, 0:T]).then_inc(taken, 1)
                    if n < HEADS:
                        dve.wait_ge(stage("dsa_exp"), n + 1)
                        steps.link(nc.vector.reciprocal(small[:, st + 4:st + 6], small[:, st + 2:st + 4]))
                        for t, (a, b) in enumerate(cut):
                            m = ts(p_[:, a:b], p_[:, a:b], small[:, st + 4 + t:st + 5 + t], None, ALU.mult)
                            if t == 0:
                                steps.mark(m)
                        m.then_inc(stage("dsa_p"), 1)
                    if n >= 2:
                        h_low(h0 + 13, n - 2)
                add_out(i, ns + 9)

            def attn(i, name, prm):
                ns, h0, l = starts[i]["ns"], before(i, "h"), prm["l"]
                bk = lambda label: wrk[:, use[name, label] % BANKS, :]
                full = lambda label: wait_full(dve, name, label)
                after = lambda label: dve.wait_ge(taken, use[name, label] + 1)
                half = lambda label: bk(label).rearrange("p (a b) -> p a b", b=T)
                split_to(ns + 1)
                normed(i, dict(prm, x="c"), src=(c,))
                split_to(ns + 2)
                lam = col("diff_lambda", 0, 256).rearrange("p (a b) -> p a b", b=64)
                prod = a_tmp[:, 0:P].rearrange("p (a b) -> p a b", b=64)
                steps.link(tt(prod, lam[:, 0:4:2, :], lam[:, 1:4:2, :], ALU.mult))
                nc.vector.tensor_reduce(small[:, 60:62], prod, AX.X, ALU.add).then_inc(stage("at_lam"), 1)

                def place(q, label):
                    full(label)
                    p = int(label[-1])
                    side = 1 if "c" in label else 0
                    if label[0] == "v":
                        v = n_v if label[1] == "a" else f_v
                        dst, src = v[:, 2 * side:2 * side + 2, p * 256:(p + 1) * 256], bk(label).rearrange("p (a b) -> p a b", b=256)
                    elif label[0] == "k":
                        dst, src = (n_k if label[1] == "a" else f_k)[:, 2 * p:2 * p + 2, side * T:(side + 1) * T], half(label)
                    else:
                        dst, src = (n_q if label[1] == "a" else f_q)[:, 2 * p:2 * p + 2, :], half(label)
                    dve.wait_ge(taken, use[name, label])
                    ts(dst, src, 0.125 if label[0] == "q" else 1.0, None, ALU.mult).then_inc(taken, 1)
                    split_to(ns + q + 3)

                for q, label in enumerate(CTX_PROJ):
                    if q == 5:
                        normed(i, prm, nth=1, low=False)
                    place(q, label)
                for k in range(KC):
                    h_low(h0 + 8, k)
                rot = lambda v, label: rotate([v(0), v(1)], bk(label), [cst("sin_d")] * 2, [cst("cos_d")] * 2,
                                              use[name, label] + 1, a_tmp).then_inc(stage("at_rot"), 1)
                for q, label in enumerate(LAT_PROJ):
                    place(8 + q, label)
                    if label == "kb1":
                        for p in range(2):
                            full(f"rq{p}")
                            rot(lambda k: f_q[:, 2 * p + k, :], f"rq{p}")
                            dve.wait_ge(stage("at_rot"), p + 1)
                for p in range(2):
                    full(f"rk{p}")
                    rot(lambda k: f_k[:, 2 * p + k, 0:T], f"rk{p}")
                    dve.wait_ge(stage("at_rot"), p + 3)
                dve.wait_ge(stage("at_lam_e"), 1)
                steps.link(tt(small[:, 59:60], small[:, 63:64], small[:, 62:63], ALU.subtract))
                steps.mark(ts(small[:, 59:60], small[:, 59:60], -0.2, None, ALU.add))
                steps.link(ts(small[:, 58:59], col("diff_subln_g"), 1.0 - 0.2, None, ALU.mult))
                split_to(ns + 22)
                for n in range(len(UNITS) + 2):
                    st = 32 + 8 * (n % 2)
                    two = n < NDIFF
                    if n < len(UNITS):
                        for m, label in enumerate([f"s{n}"] + [f"r{n}"] * two):
                            full(label)
                            mx = nc.vector.tensor_reduce(small[:, st + m:st + m + 1], bk(label), AX.X, ALU.max, negate=True)
                            if m == 0 and two:
                                steps.mark(mx)
                        mx.then_inc(stage("at_max"), 1)
                    if n >= 2:
                        kind, hd, t = UNITS[n - 2]
                        full(f"o{n - 2}")
                        dve.wait_ge(taken, use[name, f"o{n - 2}"])
                        r = slice(0, P) if kind == "diff" else slice(64 * (hd % 2), 64 * (hd % 2) + 64)
                        k = hd if kind == "diff" else 4 + hd // 2
                        nc.vector.tensor_copy(h[r, k, t * P:(t + 1) * P], bk(f"o{n - 2}")[r, 0:P]).then_inc(taken, 1)
                    if n < len(UNITS):
                        after(f"r{n}" if two else f"s{n}")
                        p_ = a_p[:, n % 3, :]
                        steps.link(nc.vector.reciprocal(small[:, st + 4:st + 5 + two], small[:, st + 2:st + 3 + two]))
                        if two:
                            steps.mark(tt(small[:, st + 6:st + 7], small[:, st + 5:st + 6], small[:, 59:60], ALU.mult))
                            steps.link(ts(p_, p_, small[:, st + 4:st + 5], None, ALU.mult))
                            stt(p_, a_p1[:, n % 2, :], small[:, st + 6:st + 7], p_, ALU.mult, ALU.add).then_inc(stage("at_p"), 1)
                        else:
                            ts(p_, p_, small[:, st + 4:st + 5], None, ALU.mult).then_inc(stage("at_p"), 1)
                    if n == SUBLN + 1:
                        dve.wait_ge(stage("at_rr"), 1)
                        v = h[:, 0:4, :].rearrange("p a b -> p (a b)")
                        stt(v, v, small[:, 58:59], f_rr, ALU.mult, ALU.mult).then_inc(stage("at_d"), 1)
                        dve.wait_ge(h_hi_ready, h0 + 20)
                        tt(h_lo[:, 0:4, :], h[:, 0:4, :], h_hi[:, 0:4, :].bitcast(F32), ALU.subtract).then_inc(h_lo_ready, 4)
                    if n >= NDIFF + 2 and (n - 2 - NDIFF) % 4 == 3:
                        h_low(h0 + 16, 4 + (n - 2 - NDIFF) // 4)
                add_out(i, ns + 20, gate=lambda k: der[:, l, 0, 5 * KC + k:5 * KC + k + 1])

            def conv(i, name, prm):
                ns, h0, l = starts[i]["ns"], before(i, "h"), prm["l"]
                bk = lambda label: wrk[:, use[name, label] % BANKS, :]
                tap = lambda t, k: col("conv_w", t * KC + k)
                split_to(ns + 1)
                normed(i, prm)
                split_to(ns + 2)
                for p in range(4):
                    wait_full(dve, name, f"hh{p}")
                    dve.wait_ge(taken, use[name, f"hh{p}"])
                    u = v_u[:, p % 2, :, :]
                    tt(u, v_cg[:, p % 2, :, :], bk(f"hh{p}").rearrange("p (a b) -> p a b", b=T), ALU.mult).then_inc(taken, 1)
                    dve.wait_ge(taken, use[name, f"hh{p}"] + 1)
                    for t, (a, b) in ((1, (0, 0)), (0, (1, 0)), (2, (0, 1))):
                        for k in range(2):
                            src, dst = u[:, k, b:T - a], v_v[:, k, a:T - b]
                            if t == 1:
                                steps.mark(ts(dst, src, tap(t, 2 * p + k), None, ALU.mult))
                            else:
                                dve.wait_ge(dve_steps, steps.n - 1)
                                steps.mark(stt(dst, src, tap(t, 2 * p + k), dst, ALU.mult, ALU.add))
                    split_to(ns + 3 * p + 3)
                    split_to(ns + 3 * p + 4)
                    dve.wait_ge(taken, use[name, f"bg{p}"] + 1)
                    steps.wait()
                    tt(h[:, 2 * p:2 * p + 2, :], v_v, v_bg[:, p % 2, :, :], ALU.mult).then_inc(h_ready, 2)
                    if p < 3:
                        split_to(ns + 3 * p + 5)
                split_to(ns + 13)
                for k in range(KC):
                    h_low(h0 + 8, k)
                add_out(i, ns + 12, gate=lambda k: der[:, l, 0, 5 * KC + k:5 * KC + k + 1])

            dve.wait_ge(loaded, 16 * LOADS)
            for i, (kind, name, prm) in enumerate(ops):
                dict(ffn=ffn, mod=mod, final=final, gdn=gdn, sb=sb, dsa=dsa, attn=attn, conv=conv
                     )[kind](i, name, prm)

        @block.gpsimd
        def _(pool):
            def gdn(i, name, prm):
                g = before(i, "gdn_ops")
                for half in range(2):
                    k = 2 * g + half
                    pool.wait_ge(stage("gdn_u1"), k + 1)
                    for lv in range(len(LEVELS)):
                        if lv >= 2:
                            u = use[name, f"X{half}{lv - 2}B"]
                            wait_full(pool, name, f"X{half}{lv - 2}B")
                        nc.gpsimd.tensor_tensor(g_lts[:, lv % 2], g_lt, cst("levels", (lv + 1) * P, (lv + 2) * P).unsqueeze(1).to_broadcast([P, 8, P]),
                                                ALU.mult).then_inc(stage("gdn_lts"), 1)

            for i, (kind, name, prm) in enumerate(ops):
                if kind == "gdn":
                    gdn(i, name, prm)

        @block.gpsimd
        def _(pool):
            for i, (kind, name, prm) in enumerate(ops):
                if kind != "attn":
                    continue
                came = [sem(f"bias_landed{q}") for q in range(4)]
                pool.wait_ge(loaded, 16 * LOADS)
                pool.wait_ge(h_ready, h_writes(before(i, "h")) + KC)

                def load(n):
                    if n >= 4:
                        wait_full(pool, name, f"s{UNITS.index(('near', n - 4, 1))}")
                    pool.dma_start(n_bias[:, 2 * (n % 4):2 * (n % 4) + 2, :], bias_d[n]).then_inc(came[n % 4], 16)

                for n in range(4):
                    load(n)
                for n in range(HEADS):
                    pool.wait_ge(came[n % 4], 16 * (n // 4 + 1))
                    b = n_bias[:, 2 * (n % 4):2 * (n % 4) + 2, :]
                    mask = cst("na_mask")[:, 0:T].unsqueeze(1).to_broadcast([P, 2, T])
                    nc.gpsimd.tensor_tensor(b, b, mask, ALU.add).then_inc(stage("at_bias"), 1)
                    if n >= 3 and n + 1 < HEADS:
                        load(n + 1)


def chunks(v):
    return np.asarray(v).reshape(-1, P).T


def pieces(w):
    k, n = w.shape
    p = w.reshape(k // P, P, n // 256, 256).transpose(2, 1, 0, 3).reshape(n // 256, P, -1)
    return np.pad(p, ((0, 0), (0, 0), (0, PW - p.shape[2])))


def flat_piece(w):
    p = w.reshape(w.shape[0] // P, P, w.shape[1]).transpose(1, 0, 2).reshape(1, P, -1)
    return np.pad(p, ((0, 0), (0, 0), (0, PW - p.shape[2])))


def ffn_pieces(gate, up, down):
    g, u = pieces(gate), pieces(up)
    d = down.reshape(STEPS, 2, P, D).transpose(0, 2, 1, 3).reshape(STEPS, P, PW)
    order = [g[0:1], u[0:1]]
    for s in range(1, STEPS):
        order += [g[s:s + 1], u[s:s + 1], d[s - 1:s]]
    return order + [d[STEPS - 1:]]


def constants():
    a = {}
    i, j = np.arange(P)[:, None], np.arange(P)[None, :]
    a["ident"] = i == j
    a["ones"] = np.ones((P, P))
    a["half_ones"] = (i // 64) == (j // 64)
    a["suffix"] = i > j
    a["causal"] = i <= j
    a["strict"] = i < j
    lv = [(i // s + 1 == j // s) & ((j // s) % 2 == 1) for s in [1] + LEVELS]
    a["levels"] = np.concatenate(lv, 1)

    def rope(pairs, ang):
        swap, cos, sin = np.zeros((P, P)), np.ones((P, T)), np.zeros((P, T))
        for (lo, hi), g in zip(pairs, ang):
            swap[hi, lo], swap[lo, hi] = -1.0, 1.0
            cos[lo] = cos[hi] = np.cos(g)
            sin[lo] = sin[hi] = np.sin(g)
        return swap, cos, sin

    pos = np.arange(T, dtype=np.float32)

    def angles(r):
        inv = (np.float32(500000.0) ** (-np.arange(r // 2, dtype=np.float32) * np.float32(2.0 / r))).astype(np.float32)
        return [(pos * f).astype(np.float32).astype(np.float64) for f in inv]

    a["rope_q"], a["cos_q"], a["sin_q"] = rope([(f, f + 16) for f in range(16)], angles(32))
    two = [(64 * m + f, 64 * m + f + 8) for m in range(2) for f in range(8)]
    a["rope_i"], a["cos_i"], a["sin_i"] = rope(two, angles(16) * 2)
    inv = (np.float32(10000.0) ** (-np.arange(16, dtype=np.float32) / np.float32(16))).astype(np.float32)
    row, colm = (np.arange(T) // 64).astype(np.float32), (np.arange(T) % 64).astype(np.float32)
    ang = [(row * f).astype(np.float32).astype(np.float64) for f in inv] + [(colm * f).astype(np.float32).astype(np.float64) for f in inv]
    two = [(64 * m + 2 * f, 64 * m + 2 * f + 1) for m in range(2) for f in range(32)]
    a["rope_d"], a["cos_d"], a["sin_d"] = rope(two, ang * 2)
    q = np.arange(P)[:, None]
    k = np.arange(T)[None, :]
    a["above"] = np.concatenate([k <= q, k <= q + P], 1)
    qc, kc = np.arange(64), np.arange(64)
    start = np.clip(qc - 8, 0, 48)
    ok = (kc[None] >= start[:, None]) & (kc[None] < start[:, None] + 16)
    a["na_mask"] = np.tile(np.where(ok, 0.0, -1e30), (2, 8))
    return np.concatenate([np.asarray(a[k], np.float32)[:, :w] for k, w in CONST_WIDTHS.items()], 1)


def vectors(a):
    v = {}
    for i in range(4):
        v[f"ffn1_norm{i}"], v[f"mix_norm{i}"], v[f"ffn2_norm{i}"] = (chunks(a[n][i]) for n in ("ffn1_norm", "mix_norm", "ffn2_norm"))
    v["final_norm"], v["final_g"] = chunks(a["final_norm"]), chunks(a["final_g_2"])
    v["c"] = np.stack([chunks(a["c_2"]), chunks(a["c_ctx_2"])], 2).reshape(P, -1)
    for l in range(2):
        v[f"mod_b{l}"] = chunks(a["mod_b_2"][l])
        for s in range(3):
            v[f"norm_g{l}{s}"] = chunks(a["norm_g_2"][l, s])
    pad = lambda t: np.pad(t, (0, P - len(t)))[:, None]
    for g in range(2):
        v[f"gdn_conv{g}"] = chunks(a["gdn_conv"][g])
        v[f"gdn_norm{g}"] = a["gdn_norm"][g][:, None]
        v[f"gdn_a_log{g}"], v[f"gdn_dt_bias{g}"] = pad(a["gdn_a_log"][g]), pad(a["gdn_dt_bias"][g])
    v["dsa_cq_norm"], v["dsa_ckv_norm"] = chunks(a["dsa_cq_norm"]), chunks(a["dsa_ckv_norm"])
    v["dsa_kidx_norm"] = np.tile(a["dsa_kidx_norm"][0], 2)[:, None]
    v["diff_subln_g"] = a["diff_subln_g_2"][0][:, None]
    v["diff_lambda"] = np.broadcast_to(a["diff_lambda_2"].reshape(1, 256), (P, 256))
    v["conv_w"] = chunks(a["conv_w_2"])
    return np.concatenate([v[n].reshape(P, w) for n, (_, w) in COL.items()], 1)


def weights_of(kind, name, prm, a):
    i = int(name[-1]) if name[-1].isdigit() else 0
    if kind == "ffn" and name.startswith("ffn"):
        n = name[:4]
        gu = a[f"{n}_w_gu"][i]
        return ffn_pieces(gu[:, :F], gu[:, F:], a[f"{n}_w_down"][i])
    if kind == "ffn":
        l, f = prm["l"], prm["s"] // 2
        return ffn_pieces(a["ffn_w_gate_2"][l, f], a["ffn_w_up_2"][l, f], a["ffn_w_down_2"][l, f])
    if kind == "mod":
        return [pieces(a["mod_w_2"][prm["l"]])]
    if kind == "final":
        return []
    return MIXER_WEIGHTS[kind](prm, a)


MIXER_WEIGHTS = {}


def gdn_weights(prm, a):
    w, w_out = a["gdn_w_in"][prm["j"]], a["gdn_w_out"][prm["j"]]
    n = HEADS * HD
    gates = np.zeros((D, 256), np.float32)
    gates[:, 0:8], gates[:, 32:40] = w[:, 4 * n + HEADS:], w[:, 4 * n:4 * n + HEADS]
    return [pieces(gates), pieces(w[:, :4 * n]), pieces(w_out)]


MIXER_WEIGHTS["gdn"] = gdn_weights


def dsa_weights(prm, a):
    j = prm["j"]
    w = a["dsa_w_in"][j]
    proj = np.zeros((D, 8 * P), np.float32)
    proj[:, 0:640] = w[:, 0:640]
    proj[:, 640:672] = w[:, 640:672]
    proj[:, 768:832] = proj[:, 832:896] = w[:, 672:736]
    proj[:, 896:904] = w[:, 736:744]
    uk = np.zeros((256, HEADS, P), np.float32)
    uk[:, :, 32:] = a["dsa_w_uk"][j].reshape(256, HEADS, 96)
    uq = a["dsa_w_uq"][j]
    return [pieces(proj), flat_piece(a["dsa_w_qidx"][j]), flat_piece(uq[:, 0:512]), flat_piece(uq[:, 512:1024]),
            flat_piece(uk.reshape(256, D)), flat_piece(a["dsa_w_uv"][j]), pieces(a["dsa_w_out"][j])]


MIXER_WEIGHTS["dsa"] = dsa_weights


def conv_weights(prm, a):
    w = pieces(a["conv_w_in_2"][0])
    return [w[k * 4 + p:k * 4 + p + 1] for p in range(4) for k in (1, 2, 0)] + [pieces(a["conv_w_out_2"][0])]




def attn_weights(prm, a):
    w, w_out = pieces(a["attn_w_in_2"][0]), a["attn_w_out_2"][0]
    two = lambda j: w[2 * j:2 * j + 2]
    return [two(j) for j in (1, 2, 4, 5, 0, 1, 2, 3, 4, 5)] + [pieces(np.concatenate([w_out[512:], w_out[:512]]))]


MIXER_WEIGHTS["attn"] = attn_weights
MIXER_WEIGHTS["conv"] = conv_weights
MIXER_WEIGHTS["sb"] = lambda prm, a: [pieces(a["sb_w_in"][prm["j"]]), pieces(a["sb_w_out"][prm["j"]])]



def rel_bias(rpb):
    t = np.arange(T)
    row, at = t // 64, t % 64
    dr = row[None, :] - row[:, None] + 7
    dc = np.clip(at[None, :] - at[:, None] + 15, 0, 30)
    b = rpb[:, dr, dc]
    return np.ascontiguousarray(b.reshape(HEADS, 2, P, T).transpose(0, 2, 1, 3).reshape(HEADS, P, 2 * T))


def kernel(**inputs):
    import concourse.bacc as bacc
    from concourse.bass_utils import run_bass_kernel_spmd

    a = {k: np.asarray(v) for k, v in inputs.items()}
    feature_major = lambda t: np.ascontiguousarray(t[0].T.reshape(KC, P, T).transpose(1, 0, 2))
    arrays = dict(
        wts=np.concatenate([w for kind, name, prm in OPS for w in weights_of(kind, name, prm, a)]),
        vec=np.ascontiguousarray(vectors(a)),
        const=constants(),
        x=feature_major(a["x"]),
        c=feature_major(a["ctx_2"]),
        bias=rel_bias(a["na_rpb_2"][0]),
    )
    nc = bacc.Bacc("TRN2", target_bir_lowering=False, num_devices=1)
    tensors = [nc.dram_tensor(f"in_{n}", v.shape, F32, kind="ExternalInput").ap() for n, v in arrays.items()]
    out = nc.dram_tensor("out", (P, KC, T), F32, kind="ExternalOutput").ap()
    build(nc, *tensors, out, OPS)
    r = run_bass_kernel_spmd(nc, [{f"in_{n}": v for n, v in arrays.items()}], core_ids=[0])
    return r.results[0]["out"].transpose(1, 0, 2).reshape(D, T).T[None]
```
